# Optimizing a Trainium2 kernel written in Bass

```python
import jax, jax.numpy as jnp
from jax import lax
import numpy as np

D_MODEL = 2048
BATCH = 1
SEQ = 256
DEPTH = 2

CHUNK = 64
EPS = 1e-6
D_POOL = D_MODEL // 2
POOL_WINDOWS = (2, 4, 8, 16)
N_POOL_GROUPS = len(POOL_WINDOWS)
POOL_GROUP = D_POOL // N_POOL_GROUPS
D_CONV = D_MODEL // 2
CONV_K = 31
D_AB_IN = D_POOL + 2 * D_CONV
D_SHORT = D_MODEL
SHORT_K = 3
D_FF = 4 * D_MODEL

N_EVEN = (DEPTH + 1) // 2
N_ODD = DEPTH // 2


def rms_norm(x, g):
    xf = x.astype(jnp.float32)
    y = xf * lax.rsqrt(jnp.mean(xf * xf, axis=-1, keepdims=True) + EPS)
    return (y * g.astype(jnp.float32)).astype(x.dtype)

def layer_norm(x, g, b):
    xf = x.astype(jnp.float32)
    mu = jnp.mean(xf, axis=-1, keepdims=True)
    xc = xf - mu
    var = jnp.mean(xc * xc, axis=-1, keepdims=True)
    y = xc * lax.rsqrt(var + EPS) * g.astype(jnp.float32) + b.astype(jnp.float32)
    return y.astype(x.dtype)

def causal_depthwise_conv(u, w):
    k = w.shape[0]
    return lax.conv_general_dilated(
        u, w[:, None, :].astype(u.dtype), window_strides=(1,), padding=[(k - 1, 0)],
        dimension_numbers=("NWC", "WIO", "NWC"), feature_group_count=u.shape[-1])

def multiscale_pool(u, pool_w, pool_scale):
    b, t, _ = u.shape
    uf = u.astype(jnp.float32)
    csp = jnp.pad(jnp.cumsum(uf, axis=1), ((0, 0), (1, 0), (0, 0)))
    n_valid = jnp.arange(1, t + 1, dtype=jnp.float32)
    means = []
    for g, w in enumerate(POOL_WINDOWS):
        c = csp[..., g * POOL_GROUP:(g + 1) * POOL_GROUP]
        lag = jnp.pad(c, ((0, 0), (w - 1, 0), (0, 0)))[:, :t]
        cnt = jnp.minimum(n_valid, float(w))[None, :, None]
        means.append((c[:, 1:] - lag) / cnt)
    pooled = (jnp.concatenate(means, axis=-1) - uf).astype(u.dtype)
    pooled = pooled.reshape(b, t, N_POOL_GROUPS, POOL_GROUP)
    mixed = jnp.einsum("btgc,gce->btge", pooled, pool_w).reshape(b, t, D_POOL)
    return mixed * pool_scale

def pool_conformer_mixer(h, w_in, pool_w, pool_scale, conv_w, conv_b, ln_g, ln_b, w_out):
    z = jnp.einsum("btd,de->bte", h, w_in)
    u_pool = z[..., :D_POOL]
    v = z[..., D_POOL:D_POOL + D_CONV]
    gate = z[..., D_POOL + D_CONV:]
    y_pool = multiscale_pool(u_pool, pool_w, pool_scale)
    c = causal_depthwise_conv(v * jax.nn.sigmoid(gate), conv_w) + conv_b
    y_conv = jax.nn.silu(layer_norm(c, ln_g, ln_b))
    y = jnp.concatenate([y_pool, y_conv], axis=-1)
    return jnp.einsum("bte,ed->btd", y, w_out)

def short_conv_mixer(h, w_in, conv_w, w_out):
    z = jnp.einsum("btd,de->bte", h, w_in)
    b_gate = z[..., :D_SHORT]
    c_gate = z[..., D_SHORT:2 * D_SHORT]
    u = z[..., 2 * D_SHORT:]
    y = b_gate * causal_depthwise_conv(c_gate * u, conv_w)
    return jnp.einsum("bte,ed->btd", y, w_out)

def sq_relu_mlp(h, w1, w2):
    a = jax.nn.relu(jnp.einsum("btd,df->btf", h, w1))
    return jnp.einsum("btf,fd->btd", a * a, w2)

def first_inputs(seed: int = 0) -> dict:
    key = jax.random.key(seed)
    ks = jax.random.split(key, 20)
    f32 = jnp.float32

    def nrm(k, shape, scale):
        return jax.random.normal(k, shape, f32) * scale

    def gain(k, shape):
        return 1.0 + 0.02 * jax.random.normal(k, shape, f32)

    return {
        "x": jax.random.normal(ks[0], (BATCH, SEQ, D_MODEL), f32),
        "mix_pre_g": gain(ks[1], (DEPTH, D_MODEL)),
        "mix_post_g": gain(ks[2], (DEPTH, D_MODEL)),
        "ffn_pre_g": gain(ks[3], (DEPTH, D_MODEL)),
        "ffn_post_g": gain(ks[4], (DEPTH, D_MODEL)),
        "ab_w_in": nrm(ks[5], (N_EVEN, D_MODEL, D_AB_IN), D_MODEL ** -0.5),
        "pool_w": nrm(ks[6], (N_EVEN, N_POOL_GROUPS, POOL_GROUP, POOL_GROUP), POOL_GROUP ** -0.5),
        "pool_scale": 1.0 + 0.1 * jax.random.normal(ks[7], (N_EVEN, D_POOL), f32),
        "conv_w": nrm(ks[8], (N_EVEN, CONV_K, D_CONV), CONV_K ** -0.5),
        "conv_b": nrm(ks[9], (N_EVEN, D_CONV), 0.02),
        "conv_ln_g": gain(ks[10], (N_EVEN, D_CONV)),
        "conv_ln_b": nrm(ks[11], (N_EVEN, D_CONV), 0.02),
        "ab_w_out": nrm(ks[12], (N_EVEN, D_POOL + D_CONV, D_MODEL), (D_POOL + D_CONV) ** -0.5),
        "sc_w_in": nrm(ks[13], (N_ODD, D_MODEL, 3 * D_SHORT), D_MODEL ** -0.5),
        "sc_conv_w": nrm(ks[14], (N_ODD, SHORT_K, D_SHORT), SHORT_K ** -0.5),
        "sc_w_out": nrm(ks[15], (N_ODD, D_SHORT, D_MODEL), D_SHORT ** -0.5),
        "ffn_w1": nrm(ks[16], (DEPTH, D_MODEL, D_FF), D_MODEL ** -0.5),
        "ffn_w2": nrm(ks[17], (DEPTH, D_FF, D_MODEL), D_FF ** -0.5),
    }

def first_block(x, mix_pre_g, mix_post_g, ffn_pre_g, ffn_post_g, ab_w_in, pool_w, pool_scale,
              conv_w, conv_b, conv_ln_g, conv_ln_b, ab_w_out, sc_w_in, sc_conv_w, sc_w_out,
              ffn_w1, ffn_w2):
    for layer in range(DEPTH):
        i = layer // 2
        h = rms_norm(x, mix_pre_g[layer])
        if layer % 2 == 0:
            m = pool_conformer_mixer(h, ab_w_in[i], pool_w[i], pool_scale[i], conv_w[i], conv_b[i],
                                     conv_ln_g[i], conv_ln_b[i], ab_w_out[i])
        else:
            m = short_conv_mixer(h, sc_w_in[i], sc_conv_w[i], sc_w_out[i])
        x = x + rms_norm(m, mix_post_g[layer])
        h = rms_norm(x, ffn_pre_g[layer])
        x = x + rms_norm(sq_relu_mlp(h, ffn_w1[layer], ffn_w2[layer]), ffn_post_g[layer])
    return x


DEPTH_2 = 1

N_ATT_HEADS = 8
HEAD_DIM = 128
ATT_WIDTH = N_ATT_HEADS * HEAD_DIM
MOBA_BLOCK = 256
MOBA_TOPK = 3
Q_CHUNK = 128
N_SGU_GROUPS = 8
SGU_GROUP_DIM = 128
SGU_WIDTH = N_SGU_GROUPS * SGU_GROUP_DIM
SGU_CHUNK = 128
IN_SPLITS = (ATT_WIDTH, ATT_WIDTH, ATT_WIDTH, ATT_WIDTH,
             SGU_WIDTH, SGU_WIDTH, SGU_WIDTH,
             D_MODEL, D_MODEL)
IN_WIDTH = 4 * ATT_WIDTH + 3 * SGU_WIDTH + 2 * D_MODEL
NEG_INF = -1e30


def rms_norm_2(x, g):
    xf = x.astype(jnp.float32)
    y = xf * lax.rsqrt(jnp.mean(xf * xf, axis=-1, keepdims=True) + EPS)
    return (y * g.astype(jnp.float32)).astype(x.dtype)

def moba_attention(q, k, v):
    B, S, H, Dh = q.shape
    nb = -(-S // MOBA_BLOCK)
    s_pad = nb * MOBA_BLOCK
    topk = min(MOBA_TOPK, nb)
    nc = S // Q_CHUNK
    scale = Dh ** -0.5

    qh = q.transpose(0, 2, 1, 3)
    pad = ((0, 0), (0, 0), (0, s_pad - S), (0, 0))
    kh = jnp.pad(k.transpose(0, 2, 1, 3), pad)
    vh = jnp.pad(v.transpose(0, 2, 1, 3), pad)
    k_blocks = kh.reshape(B, H, nb, MOBA_BLOCK, Dh)
    v_blocks = vh.reshape(B, H, nb, MOBA_BLOCK, Dh)
    k_mean = jnp.mean(k_blocks.astype(jnp.float32), axis=3)
    q_chunks = qh.reshape(B, H, nc, Q_CHUNK, Dh).transpose(2, 0, 1, 3, 4)

    bi = jnp.arange(B)[:, None, None, None]
    hi = jnp.arange(H)[None, :, None, None]
    blk_ids = jnp.arange(nb)

    def one_chunk(args):
        qc, c = args
        q_pos = c * Q_CHUNK + jnp.arange(Q_CHUNK)
        cur = (c * Q_CHUNK) // MOBA_BLOCK
        gate = jnp.einsum('bhqd,bhnd->bhqn', qc.astype(jnp.float32), k_mean)
        gate = jnp.where(blk_ids < cur, gate, NEG_INF)
        _, idx = lax.top_k(gate, topk)
        valid = idx < cur
        k_sel = k_blocks[bi, hi, idx]
        v_sel = v_blocks[bi, hi, idx]
        s_past = jnp.einsum('bhqd,bhqknd->bhqkn', qc, k_sel,
                            preferred_element_type=jnp.float32) * scale
        s_past = jnp.where(valid[..., None], s_past, NEG_INF)
        k_own = lax.dynamic_index_in_dim(k_blocks, cur, axis=2, keepdims=False)
        v_own = lax.dynamic_index_in_dim(v_blocks, cur, axis=2, keepdims=False)
        s_own = jnp.einsum('bhqd,bhnd->bhqn', qc, k_own,
                           preferred_element_type=jnp.float32) * scale
        key_pos = cur * MOBA_BLOCK + jnp.arange(MOBA_BLOCK)
        s_own = jnp.where(key_pos[None, :] <= q_pos[:, None], s_own, NEG_INF)
        logits = jnp.concatenate(
            [s_past.reshape(B, H, Q_CHUNK, topk * MOBA_BLOCK), s_own], axis=-1)
        p = jax.nn.softmax(logits, axis=-1)
        p_past = p[..., :topk * MOBA_BLOCK].reshape(B, H, Q_CHUNK, topk, MOBA_BLOCK)
        p_own = p[..., topk * MOBA_BLOCK:]
        o = (jnp.einsum('bhqkn,bhqknd->bhqd', p_past.astype(v_sel.dtype), v_sel)
             + jnp.einsum('bhqn,bhnd->bhqd', p_own.astype(v_own.dtype), v_own))
        return o.astype(qc.dtype)

    out = lax.map(one_chunk, (q_chunks, jnp.arange(nc, dtype=jnp.int32)))
    return out.transpose(1, 0, 3, 2, 4).reshape(B, S, H * Dh)

def spatial_gating(u, v, v_norm_g, w_s, b_s):
    B, S, _ = u.shape
    n = S // SGU_CHUNK
    vg = rms_norm_2(v.reshape(B, S, N_SGU_GROUPS, SGU_GROUP_DIM), v_norm_g)
    vg = vg.reshape(B, n, SGU_CHUNK, N_SGU_GROUPS, SGU_GROUP_DIM)
    causal = jnp.tril(jnp.ones((SGU_CHUNK, SGU_CHUNK), dtype=bool))
    w = jnp.where(causal[None], w_s, jnp.zeros((), w_s.dtype))
    mixed = jnp.einsum('gts,bnsgc->bntgc', w, vg) + b_s.T[:, :, None]
    return u * mixed.reshape(B, S, SGU_WIDTH)

def hybrid_layer(x, norm_g, w_in, q_norm_g, k_norm_g, sgu_norm_g, w_s, b_s,
                 w_proj_a, w_proj_b, w_out):
    B, S, _ = x.shape
    h = rms_norm_2(x, norm_g)
    proj = h @ w_in
    cuts = [int(c) for c in np.cumsum(IN_SPLITS)[:-1]]
    q, k, v, z_a, u_b, v_b, z_b, g_a, g_b = jnp.split(proj, cuts, axis=-1)
    q = rms_norm_2(q.reshape(B, S, N_ATT_HEADS, HEAD_DIM), q_norm_g)
    k = rms_norm_2(k.reshape(B, S, N_ATT_HEADS, HEAD_DIM), k_norm_g)
    v = v.reshape(B, S, N_ATT_HEADS, HEAD_DIM)
    att = moba_attention(q, k, v)
    y_a = (att * jax.nn.silu(z_a)) @ w_proj_a
    sgu = spatial_gating(jax.nn.gelu(u_b), jax.nn.gelu(v_b), sgu_norm_g, w_s, b_s)
    y_b = (sgu * jax.nn.silu(z_b)) @ w_proj_b
    merged = jax.nn.sigmoid(g_a) * y_a + jax.nn.sigmoid(g_b) * y_b
    return x + merged @ w_out

def second_inputs(seed: int = 0) -> dict:
    key = jax.random.key(seed)
    ks = jax.random.split(key, 12)
    f32 = jnp.float32
    x = jax.random.normal(ks[0], (BATCH, SEQ, D_MODEL), f32)
    norm_g = 1.0 + 0.02 * jax.random.normal(ks[1], (DEPTH_2, D_MODEL), f32)
    w_in = jax.random.normal(ks[2], (DEPTH_2, D_MODEL, IN_WIDTH), f32) * D_MODEL ** -0.5
    q_norm_g = 1.0 + 0.02 * jax.random.normal(ks[3], (DEPTH_2, HEAD_DIM), f32)
    k_norm_g = 1.0 + 0.02 * jax.random.normal(ks[4], (DEPTH_2, HEAD_DIM), f32)
    sgu_norm_g = 1.0 + 0.02 * jax.random.normal(ks[5], (DEPTH_2, SGU_GROUP_DIM), f32)
    w_spatial = jax.random.normal(ks[6], (DEPTH_2, N_SGU_GROUPS, SGU_CHUNK, SGU_CHUNK), f32) * SGU_CHUNK ** -0.5
    b_spatial = 1.0 + 0.1 * jax.random.normal(ks[7], (DEPTH_2, N_SGU_GROUPS, SGU_CHUNK), f32)
    w_proj_a = jax.random.normal(ks[8], (DEPTH_2, ATT_WIDTH, D_MODEL), f32) * ATT_WIDTH ** -0.5
    w_proj_b = jax.random.normal(ks[9], (DEPTH_2, SGU_WIDTH, D_MODEL), f32) * SGU_WIDTH ** -0.5
    w_out = jax.random.normal(ks[10], (DEPTH_2, D_MODEL, D_MODEL), f32) * D_MODEL ** -0.5
    return {"x": x, "norm_g": norm_g, "w_in": w_in, "q_norm_g": q_norm_g,
            "k_norm_g": k_norm_g, "sgu_norm_g": sgu_norm_g, "w_spatial": w_spatial,
            "b_spatial": b_spatial, "w_proj_a": w_proj_a, "w_proj_b": w_proj_b,
            "w_out": w_out}

def second_block(x, norm_g, w_in, q_norm_g, k_norm_g, sgu_norm_g, w_spatial, b_spatial,
              w_proj_a, w_proj_b, w_out):
    for l in range(DEPTH_2):
        x = hybrid_layer(x, norm_g[l], w_in[l], q_norm_g[l], k_norm_g[l], sgu_norm_g[l],
                         w_spatial[l], b_spatial[l], w_proj_a[l], w_proj_b[l], w_out[l])
    return x


def setup_inputs(seed=0):
    out = dict(first_inputs(seed))
    for name, value in second_inputs(seed + 1).items():
        if name != "x":
            out[name + "_2"] = value
    return out


def reference(
    x, mix_pre_g, mix_post_g, ffn_pre_g, ffn_post_g, ab_w_in, pool_w, pool_scale, conv_w,
    conv_b, conv_ln_g, conv_ln_b, ab_w_out, sc_w_in, sc_conv_w, sc_w_out, ffn_w1, ffn_w2,
    norm_g_2, w_in_2, q_norm_g_2, k_norm_g_2, sgu_norm_g_2, w_spatial_2, b_spatial_2,
    w_proj_a_2, w_proj_b_2, w_out_2,
):
    x = first_block(
        x, mix_pre_g, mix_post_g, ffn_pre_g, ffn_post_g, ab_w_in, pool_w, pool_scale, conv_w,
        conv_b, conv_ln_g, conv_ln_b, ab_w_out, sc_w_in, sc_conv_w, sc_w_out, ffn_w1, ffn_w2,
    )
    return second_block(
        x, norm_g_2, w_in_2, q_norm_g_2, k_norm_g_2, sgu_norm_g_2, w_spatial_2, b_spatial_2,
        w_proj_a_2, w_proj_b_2, w_out_2,
    )


_drawn_inputs = setup_inputs


def setup_inputs(seed=0):
    import zlib

    import numpy as np

    out = dict(_drawn_inputs(seed))
    spreads = {}
    factors = {'ffn_pre_g': 2.84,
     'ffn_post_g': 3.299,
     'conv_ln_g': 4.443,
     'conv_ln_b': 5.141,
     'norm_g_2': 8.0,
     'q_norm_g_2': 30.011,
     'k_norm_g_2': 30.722,
     'sgu_norm_g_2': 27.69,
     'b_spatial_2': 5.959}
    for name, (base, spread) in spreads.items():
        noise = np.random.default_rng([zlib.crc32(name.encode()), seed]).standard_normal(out[name].shape)
        drawn = base * np.exp(spread * noise) if base else spread * noise
        out[name] = __import__('jax').numpy.asarray(drawn.astype(out[name].dtype))
    for name, factor in factors.items():
        out[name] = (out[name] * factor).astype(out[name].dtype)
    return out
```

```python
import numpy as np
import concourse.bass as bass
from concourse import mybir
from concourse.alu_op_type import AluOpType as ALU
from contextlib import ExitStack

F32 = mybir.dt.float32
F32R = mybir.dt.float32r
ACT = mybir.ActivationFunctionType
AXIS = mybir.AxisListType

P = 128
TOK = 256
NT = TOK // P
D = 2048
CH = 512
GK = CH // P
NG = D // CH
EPS = 1e-6
D_POOL = 1024
D_CONV = 1024
CONV_K = 31
SHORT_K = 3
D_FF = 4 * D
FF_BLOCK = 1024
WINDOWS = (2, 4, 8, 16)
HEADS = 8
HD = 128
SCALE = float(HD) ** -0.5
GELU_A = 0.044715
GELU_B = 2.0 * (2.0 / np.pi) ** 0.5

RAW_SLOTS = 3
SPLIT_SLOTS = 4
AHEAD = SPLIT_SLOTS - 1
STEP_K = 2

ROWS = {}
_at = 0
for _name, _n in (("mix_pre0", 16), ("mix_pre1", 16), ("ffn_pre0", 16), ("ffn_pre1", 16), ("pre2", 16),
                  ("pool_scale", 8), ("conv_b", 8), ("ln_g", 8), ("ln_b", 8), ("b_spatial", 8),
                  ("q_g", 1), ("k_g", 1)):
    ROWS[_name] = _at
    _at += _n
N_ROWS = _at
CONV_ROWS = CONV_K * D_CONV // P // 2
SHORT_ROWS = SHORT_K * D // P
COL_CONV = N_ROWS
COL_SHORT = COL_CONV + 2 * CONV_ROWS
N_PAR = COL_SHORT + SHORT_ROWS


class Queue:

    def __init__(self, sem):
        self.todo, self.sem, self.seen = [], sem, {}

    def wait(self, *tokens):
        for token in tokens:
            if token is None:
                continue
            sem, value = token
            if self.seen.get(sem.name, 0) < value:
                self.seen[sem.name] = value
                self.todo.append((lambda e, s=sem.sem, v=value: e.wait_ge(s, v)))

    def op(self, emit, waits=(), sem=None):
        self.wait(*waits)
        sem = sem or self.sem
        sem.value += 1
        self.todo.append(lambda e: emit(e).then_inc(sem.sem, 1))
        return (sem, sem.value)

    def quiet(self, emit, waits=()):
        self.wait(*waits)
        self.todo.append(emit)

    def dma(self, out, in_, sem, waits=()):
        self.wait(*waits)
        sem.value += 16
        self.todo.append(lambda e: e.dma_start(out, in_).then_inc(sem.sem, 16))
        return (sem, sem.value)

    def replay(self, e):
        for emit in self.todo:
            emit(e)


class Counter:

    def __init__(self, name, sem):
        self.name, self.sem, self.value = name, sem, 0


def build(nc, t, stop=None):
    ctx = ExitStack()
    with ctx:
        def sbuf(name, cols, dt=F32):
            return ctx.enter_context(nc.sbuf_tensor(name, [P, cols], dt))

        def counter(name):
            return Counter(name, ctx.enter_context(nc.semaphore(name)))

        x = sbuf("x_res", NT * D)[:, :].rearrange("p (t d) -> p t d", t=NT)
        acc_flat = sbuf("acc", NT * D)[:, :]
        acc = acc_flat.rearrange("p (t d) -> p t d", t=NT)
        gain_row = sbuf("gain_row", D)[:, :]
        conv_in_flat = sbuf("conv_in", 8 * (TOK + CONV_K - 1))[:, :]
        conv_out_flat = sbuf("conv_out", 8 * TOK)[:, :]
        par = sbuf("par", N_PAR)[:, :]
        ident = sbuf("ident", P)[:, :]
        mask = sbuf("mask", 3 * P)[:, :]
        ws_flat = sbuf("ws_T", HEADS * HD)[:, :]
        sgu_row = sbuf("sgu_row", HD)[:, :]
        small = sbuf("small", 512)[:, :]
        neg_half = sbuf("neg_half", 16)[:, :]
        Z_SLOTS = 3
        z = sbuf("z", Z_SLOTS * NT * CH)[:, :].rearrange("p (s t c) -> p s t c", s=Z_SLOTS, t=NT)
        halves = {}
        for name in ("A", "B"):
            halves[name] = tuple(sbuf(f"{name}_{h}", D // P * TOK, F32R)[:, :].rearrange(
                "p (k t) -> p k t", t=TOK) for h in ("hi", "lo"))
        w_raw = sbuf("w_raw", RAW_SLOTS * GK * CH)[:, :].rearrange("p (s c) -> p s c", s=RAW_SLOTS)
        w_hi = sbuf("w_hi", SPLIT_SLOTS * STEP_K * CH, F32R)[:, :].rearrange("p (s c) -> p s c", s=SPLIT_SLOTS)
        w_lo = sbuf("w_lo", SPLIT_SLOTS * STEP_K * CH, F32R)[:, :].rearrange("p (s c) -> p s c", s=SPLIT_SLOTS)
        bank = [ctx.enter_context(nc.psum_tensor(f"bank{i}", [P, CH], F32))[:, :] for i in range(8)]

        raw_loaded = [counter(f"raw_loaded{i}") for i in range(RAW_SLOTS)]
        hi_made, lo_made = counter("hi_made"), counter("lo_made")
        step_done = counter("step_done")
        x_loaded = [counter(f"x_loaded{i}") for i in range(NG)]
        par_loaded = counter("par_loaded")
        pool_w_loaded = counter("pool_w_loaded")
        gain_loaded = counter("gain_loaded")
        ws_loaded = counter("ws_loaded")
        out_written = counter("out_written")
        pe = Queue(counter("pe_did"))
        act = Queue(counter("act_did"))
        dve = Queue(counter("dve_did"))
        pool = Queue(counter("pool_did"))
        sp = Queue(counter("sp_did"))

        def a_copy(out, in_, scale=1.0, waits=(), func=ACT.Copy, sem=None):
            return act.op(lambda e: e.activation(out, in_, func, scale=scale), waits, sem)

        def a_affine(out, in_, func, scale, bias, waits=()):
            return act.op(lambda e: e.activation(out, in_, func, scale=scale, bias=bias), waits)

        def a_sum(out, in_, func, accum, waits=(), **kw):
            return act.op(lambda e: e.activation(out, in_, func, accum_out=accum, **kw), waits)

        def tt(q, out, a, b, op, waits=(), sem=None):
            return q.op(lambda e: e.tensor_tensor(out, a, b, op), waits, sem)

        def v_ts(out, a, s1, op0, s2=None, op1=None, waits=()):
            if op1 is None:
                return dve.op(lambda e: e.tensor_scalar(out, a, s1, None, op0), waits)
            return dve.op(lambda e: e.tensor_scalar(out, a, s1, s2, op0, op1), waits)

        def v_stt(out, a, s, b, op0, op1, waits=()):
            return dve.op(lambda e: e.scalar_tensor_tensor(out, a, s, b, op0, op1), waits)

        def mm(out, lhsT, rhs, start, stop, waits=()):
            pe.quiet(lambda e: e.matmul(out, lhsT, rhs, start=start, stop=stop), waits)

        def mm_last(out, lhsT, rhs, start, stop, waits=(), sem=None):
            return pe.op(lambda e: e.matmul(out, lhsT, rhs, start=start, stop=stop), waits, sem)

        def transpose(out, in_, n=P, waits=(), last=False):
            emit = lambda e: e.transpose(out, in_, ident[0:n, 0:n])
            if last:
                return pe.op(emit, waits)
            return pe.quiet(emit, waits)

        small_at = [0]

        def small_cols(n):
            at = small_at[0]
            small_at[0] += n
            assert small_at[0] <= 512
            return small[:, at:at + n]

        def inv_sqrt(out, in_, n, waits):
            w = in_.shape[-1]
            mean = small_cols(w)
            did = v_ts(mean, in_, 1.0 / n, ALU.mult, EPS, ALU.add, waits=waits)
            return tt(pool, out, mean, neg_half[:, 0:w], ALU.pow, (did,))

        bank_free = {i: () for i in range(4, 8)}
        bank_at = [0]

        def take_bank():
            i = 4 + bank_at[0] % 4
            bank_at[0] += 1
            free, bank_free[i] = bank_free[i], None
            assert free is not None, "a bank's readers are queued before it is taken again"
            return i, free

        z_free = {i: () for i in range(Z_SLOTS)}
        z_at = [0]

        def take_z():
            i = z_at[0] % Z_SLOTS
            z_at[0] += 1
            free, z_free[i] = z_free[i], None
            assert free is not None, "a slot's readers are queued before it is taken again"
            return i, free

        group_ready = {(b, g): () for b in "AB" for g in range(NG)}
        group_read = {(b, g): None for b in "AB" for g in range(NG)}

        def store_halves(buf, k, n, hi_from, lo_from):
            hi, lo = (h[:, k:k + n, :] for h in halves[buf])
            read = group_read[(buf, k // GK)]
            hi_did = hi_from(hi, (read,))
            lo_did = lo_from(lo, hi.bitcast(F32), (read, hi_did))
            group_ready[(buf, k // GK)] += (hi_did, lo_did)
            return hi_did, lo_did

        def store_scaled(buf, k, view, gains, done):
            read = group_read[(buf, k // GK)]
            hi, lo = halves[buf]
            for n in range(2):
                hi_did = a_copy(hi[:, k + n, :], view[:, n, :], gains[n], (read, done))
            for n in range(2):
                lo_did = v_stt(lo[:, k + n, :], view[:, n, :], gains[n], hi[:, k + n, :].bitcast(F32),
                               ALU.mult, ALU.subtract, (hi_did,))
            group_ready[(buf, k // GK)] += (hi_did, lo_did)
            return hi_did, lo_did

        def to_features(src, waits, evacuate):
            for half in range(2):
                i, free = take_bank()
                view = bank[i].rearrange("p (k t) -> p k t", k=2)
                did = None
                for k in range(2):
                    for tt_ in range(NT):
                        f = (2 * half + k) * P
                        did = transpose(view[:, k, tt_ * P:(tt_ + 1) * P], src(tt_)[:, f:f + P],
                                        waits=tuple(waits) + tuple(free), last=(k, tt_) == (1, NT - 1))
                bank_free[i] = tuple(evacuate(half, view, did))

        def split_plain(buf, group):
            group_ready[(buf, group)] = ()

            def evacuate(half, view, done):
                return store_halves(
                    buf, GK * group + 2 * half, 2,
                    lambda hi, w: a_copy(hi, view, waits=w + (done,)),
                    lambda lo, hi, w: tt(dve, lo, view, hi, ALU.subtract, w))
            return evacuate

        chunks = []

        def product(w, row0, nk, col0, buf, group0, done, before=None):
            chunks.append(dict(w=w, row0=row0, nk=nk, col0=col0, buf=buf, group0=group0, done=done,
                               before=before))

        later = []
        background = []
        per_step = [1]
        now = [0]

        def defer(steps, fn):
            later.append((now[0] + steps, len(later), fn))

        def run_due(everything=False):
            while True:
                due = sorted((d for d in later if everything or d[0] <= now[0]), key=lambda d: d[:2])
                if not due:
                    return
                later.remove(due[0])
                due[0][2]()

        def run_background(everything=False):
            n = len(background) if everything else min(int(per_step[0] * (now[0] + 1)) - int(per_step[0] * now[0]), len(background))
            for _ in range(n):
                background.pop(0)()

        x_ready = {(g, tt_): () for g in range(NG) for tt_ in range(NT)}
        rs = [None]
        rs_did = [None]
        post = {}

        def begin(gain_col, with_update):
            run_due(everything=True)
            run_background(everything=True)
            if with_update:
                total, factor = small_cols(NT), small_cols(NT)
                parts = post["sums"]
                did = dve.op(lambda e: e.reduce_sum(total, parts, axis=AXIS.X), post["sum_did"])
                factor_did = inv_sqrt(factor, total, D, (did,))

            def group(g):
                cols = slice(g * CH, (g + 1) * CH)
                if with_update:
                    for tt_ in range(NT):
                        x_ready[(g, tt_)] = (v_stt(x[:, tt_, cols], acc[:, tt_, cols], factor[:, tt_:tt_ + 1],
                                                   x[:, tt_, cols], ALU.mult, ALU.add,
                                                   (factor_did,) + post["gained"][(g, tt_)]),)
                group_ready[("A", g)] = ()

                def evacuate(half, view, done):
                    kt = GK * g + 2 * half
                    gains = [par[:, gain_col + kt + k:gain_col + kt + k + 1] for k in range(2)]
                    return store_scaled("A", kt, view, gains, done)
                to_features(lambda tt_: x[:, tt_, cols],
                            x_ready[(g, 0)] + x_ready[(g, 1)] + (par_did[0],), evacuate)

            def statistics():
                sums, factors = small_cols(NT), small_cols(NT)
                dids = ()
                for tt_ in range(NT):
                    waits = sum((x_ready[(g, tt_)] for g in range(NG)), ())
                    dids += (a_sum(acc[:, tt_, :], x[:, tt_, :], ACT.Square, sums[:, tt_:tt_ + 1], waits + acc_free[0]),)
                rs[0] = factors
                rs_did[0] = inv_sqrt(factors, sums, D, dids)
                acc_free[0] = dids

            group(0)
            group(1)
            defer(0, lambda: group(2))
            defer(1, lambda: group(3))
            defer(2, statistics)

        acc_free = [()]

        def add_block(n, first, ps, done):
            dids = ()
            for tt_ in range(NT):
                out = acc[:, tt_, n * CH:(n + 1) * CH]
                if first:
                    did = a_copy(out, ps[tt_], waits=(done,) + acc_free[0])
                else:
                    did = tt(dve, out, ps[tt_], out, ALU.add, (done,) + acc_did[(n, tt_)])
                acc_did[(n, tt_)] = (did,)
                dids += (did,)
            return dids

        acc_did = {}

        def finish_block(n, ps, done, alone):
            if n == 0:
                post["sums3"] = small_cols(NT * NG).rearrange("p (t n) -> p t n", t=NT)
                post["sums"], post["sum_did"], post["gained"] = post["sums3"], (), {}
            dids = ()
            for tt_ in range(NT):
                out = acc[:, tt_, n * CH:(n + 1) * CH]
                if alone:
                    did = dve.op(lambda e, o=out, i=ps[tt_]: e.tensor_copy(o, i), (done,) + acc_free[0])
                else:
                    did = tt(dve, out, ps[tt_], out, ALU.add, (done,) + acc_did[(n, tt_)])
                sq = a_sum(ps[tt_], out, ACT.Square, post["sums"][:, tt_, n:n + 1], (did,))
                gained = tt(pool, out, out, gain_row[:, n * CH:(n + 1) * CH], ALU.mult, (sq, gain_did[0]))
                post["sum_did"] += (sq,)
                post["gained"][(n, tt_)] = (gained,)
                gain_read[0] = (gained,)
                dids += (sq,)
            return dids

        gain_did, gain_read = [None], [()]

        def load_gain(src):
            gain_did[0] = sp.dma(gain_row, src.unsqueeze(0).to_broadcast([P, D]), gain_loaded, gain_read[0])

        par_did = [None]
        z_flat = [z[:, s, :, :].rearrange("p t c -> p (t c)") for s in range(Z_SLOTS)]
        rows = z_flat[0]
        act.dma(rows[0:32, 0:P], t["mix_pre_g"].rearrange("l (k p) -> (l k) p", p=P), par_loaded)
        act.dma(rows[32:64, 0:P], t["ffn_pre_g"].rearrange("l (k p) -> (l k) p", p=P), par_loaded)
        for name, key in (("norm_g_2", "pre2"), ("pool_scale", "pool_scale"), ("conv_b", "conv_b"),
                          ("conv_ln_g", "ln_g"), ("conv_ln_b", "ln_b"), ("q_norm_g_2", "q_g"),
                          ("k_norm_g_2", "k_g")):
            n = t[name].shape[1] // P
            act.dma(rows[ROWS[key]:ROWS[key] + n, 0:P], t[name].rearrange("l (k p) -> (l k) p", p=P), par_loaded)
        act.dma(rows[ROWS["b_spatial"]:ROWS["b_spatial"] + 8, 0:P], t["b_spatial_2"][0, :, :], par_loaded)
        taps = t["conv_w"].rearrange("l k (b p) -> (l k b) p", p=P)
        for h in range(2):
            act.dma(rows[0:CONV_ROWS, (1 + h) * P:(2 + h) * P], taps[h * CONV_ROWS:(h + 1) * CONV_ROWS, :], par_loaded)
        rows_did = act.dma(rows[0:SHORT_ROWS, 3 * P:4 * P], t["sc_conv_w"].rearrange("l k (b p) -> (l k b) p", p=P), par_loaded)
        sgu_did = act.dma(sgu_row, t["sgu_norm_g_2"].to_broadcast([P, HD]), ws_loaded)

        did = pool.op(lambda e: e.memset(ident, 0.0))
        ident_did = pool.op(lambda e: e.affine_select(out=ident, in_=ident, compare_op=ALU.not_equal, fill=1.0, base=0,
                                                      pattern=[[-1, P]], channel_multiplier=1), (did,))
        half_did = pool.op(lambda e: e.memset(neg_half, -0.5))

        x_dram = t["x"].rearrange("b (t p) d -> p (b t) d", p=P)
        for g in range(NG):
            did = sp.dma(x[:, :, g * CH:(g + 1) * CH], x_dram[:, :, g * CH:(g + 1) * CH], x_loaded[g])
            for tt_ in range(NT):
                x_ready[(g, tt_)] = (did,)

        i, free = take_bank()
        for b, n in enumerate((N_ROWS, CONV_ROWS, CONV_ROWS, SHORT_ROWS)):
            did = transpose(bank[i][:, b * P:b * P + n], rows[0:n, b * P:(b + 1) * P], n,
                            (ident_did, rows_did), last=b == 3)
        col, dids = 0, ()
        for b, n in enumerate((N_ROWS, CONV_ROWS, CONV_ROWS, SHORT_ROWS)):
            dids += (a_copy(par[:, col:col + n], bank[i][:, b * P:b * P + n], waits=(did,)),)
            col += n
        par_did[0] = dids[-1]
        bank_free[i] = dids
        z_free[0] = (did,)
        dve.wait(par_did[0])
        pool.wait(half_did)

        did = pool.op(lambda e: e.memset(mask, 0.0))
        mask_did = did
        for c0 in (P, 2 * P):
            mask_did = pool.op(lambda e, v=mask[:, c0:c0 + P]: e.affine_select(
                out=v, in_=v, compare_op=ALU.is_ge, fill=-1e30, base=0, pattern=[[-1, P]], channel_multiplier=1), (did,))

        conv_in = conv_in_flat.rearrange("p (b t) -> p b t", b=8)
        conv_out = conv_out_flat.rearrange("p (b t) -> p b t", b=8)
        PAD = CONV_K - 1
        pad_did = pool.op(lambda e: e.memset(conv_in[:, :, 0:PAD], 0.0))

        band0 = gain_row[:, 0:4 * TOK].rearrange("p (g t) -> p g t", g=4)
        band1 = gain_row[:, 4 * TOK:4 * TOK + 4 * P].rearrange("p (g t) -> p g t", g=4)
        band_did = ()
        for g, w in enumerate(WINDOWS):
            for band, width, edge in ((band0[:, g, :], TOK, True), (band1[:, g, :], P, False)):
                did = pool.op(lambda e, v=band, c=1.0 / w: e.memset(v, c))
                if edge:
                    for tok in range(w - 1):
                        did = pool.op(lambda e, v=band[:, tok:tok + 1], c=1.0 / (tok + 1): e.memset(v, c), (did,))
                did = pool.op(lambda e, v=band, n=width: e.affine_select(
                    out=v, in_=v, compare_op=ALU.is_ge, fill=0.0, base=0, pattern=[[1, n]], channel_multiplier=-1), (did,))
                did = pool.op(lambda e, v=band, n=width, b=w - 1: e.affine_select(
                    out=v, in_=v, compare_op=ALU.is_ge, fill=0.0, base=b, pattern=[[-1, n]], channel_multiplier=1), (did,))
                band_did += (tt(pool, band[:, 0:P], band[:, 0:P], ident, ALU.subtract, (did,)),)

        pool_w = acc_flat[:, 0:D].rearrange("p (g c e) -> p g c e", g=4, c=2)
        pool_w_did = []

        def load_pool_w():
            pool_w_did.append(sp.dma(pool_w, t["pool_w"].rearrange("l g (c p) e -> p (l g) c e", p=P),
                                     pool_w_loaded, acc_free[0]))

        state = {}

        def scaled(ps, done, func=ACT.Copy):
            s, free = take_z()
            dids = tuple(a_copy(z[:, s, tt_, :], ps[tt_], rs[0][:, tt_:tt_ + 1], (done, rs_did[0]) + free, func)
                         for tt_ in range(NT))
            return s, dids

        def l0_value(ps, done):
            state["v"] = scaled(ps, done)
            return state["v"][1]

        def l0_gate(j):
            def run(ps, done):
                v, v_did = state["v"]
                g, g_did = scaled(ps, done, ACT.Sigmoid)
                dids = tuple(tt(pool, z[:, v, tt_, :], z[:, v, tt_, :], z[:, g, tt_, :], ALU.mult,
                                (v_did[tt_], g_did[tt_])) for tt_ in range(NT))
                z_free[g] = dids

                def turn():
                    out = []

                    def evacuate(half, view, did):
                        b = GK * j + 2 * half
                        out.append(a_copy(conv_in[:, b:b + 2, PAD:], view, waits=(did, pad_did)))
                        return out[-1:]
                    to_features(lambda tt_: z[:, v, tt_, :], dids, evacuate)
                    z_free[v] = (pe.sem, pe.sem.value),
                    convolve(GK * j, tuple(out))
                defer(2, turn)
                return g_did
            return run

        conv_did = {}
        prod_buf = sbuf("tap_product", 2 * TOK)[:, :].rearrange("p (s t) -> p s t", s=2)
        tap_at = [0]
        tap_free = {0: (), 1: ()}

        def convolve(b0, ready):
            v_taps, p_taps = [], []
            for b in range(b0, b0 + 4):
                for k in range(CONV_K):
                    if b % 4 < 3:
                        v_taps.append(lambda b=b, k=k: v_tap(b, k, ready))
                    else:
                        p_taps.append(lambda b=b, k=k: p_tap(b, k, ready))
            while v_taps or p_taps:
                background.extend(v_taps[:3])
                background.extend(p_taps[:1])
                del v_taps[:3], p_taps[:1]

        def tap_cols(b, k):
            c = COL_CONV + 8 * k + b
            return conv_in[:, b, k:k + TOK], par[:, c:c + 1], conv_out[:, b, :]

        def v_tap(b, k, ready):
            src, w, out = tap_cols(b, k)
            if k == 0:
                c = ROWS["conv_b"] + b
                conv_did[b] = v_ts(out, src, w, ALU.mult, par[:, c:c + 1], ALU.add, waits=ready)
            else:
                conv_did[b] = v_stt(out, src, w, out, ALU.mult, ALU.add, (conv_did[b],))

        def p_tap(b, k, ready):
            src, w, out = tap_cols(b, k)
            if k == 0:
                c = ROWS["conv_b"] + b
                conv_did[b] = a_affine(out, src, ACT.Identity, w, par[:, c:c + 1], ready)
                return
            s = tap_at[0] % 2
            tap_at[0] += 1
            made = a_copy(prod_buf[:, s, :], src, w, tap_free[s])
            conv_did[b] = tt(pool, out, out, prod_buf[:, s, :], ALU.add, (made, conv_did[b]))
            tap_free[s] = (conv_did[b],)

        def l0_pool(j):
            def run(ps, done):
                u, u_did = scaled(ps, done)
                p_slot, p_free = take_z()
                pooled = z_flat[p_slot].rearrange("p (c t) -> p c t", c=GK)

                def windows():
                    dids = []
                    for half in range(2):
                        g = 2 * j + half
                        i, free = take_bank()
                        view = bank[i].rearrange("p (k t) -> p k t", k=2)
                        for k in range(2):
                            f = slice((2 * half + k) * P, (2 * half + k + 1) * P)
                            w = u_did + free + band_did[-1:]
                            mm(view[:, k, :], z[:, u, 0, f], band0[:, g, :], True, False, w)
                            did = mm_last(view[:, k, P:], z[:, u, 1, f], band1[:, g, :], False, True)
                        dids.append(a_copy(pooled[:, 2 * half:2 * half + 2, :], view, waits=(did,) + p_free))
                        bank_free[i] = (dids[-1],)
                    z_free[u] = ((pe.sem, pe.sem.value),)
                    gain_read[0] = ((pe.sem, pe.sem.value),)
                    defer(1, lambda: mix(dids))

                def mix(dids):
                    group_ready[("B", j)] = ()
                    for half in range(2):
                        g = 2 * j + half
                        i, free = take_bank()
                        view = bank[i].rearrange("p (k t) -> p k t", k=2)
                        for e_ in range(2):
                            for c in range(2):
                                did = mm_last(view[:, e_, :], pool_w[:, g, c, e_ * P:(e_ + 1) * P],
                                              pooled[:, 2 * half + c, :], c == 0, c == 1,
                                              (dids[half], pool_w_did[0]) + free)
                        at = ROWS["pool_scale"] + 2 * g
                        bank_free[i] = store_scaled("B", 2 * g, view, [par[:, at + c:at + c + 1] for c in range(2)], did)
                    z_free[p_slot] = ((pe.sem, pe.sem.value),)
                    acc_free[0] = ((pe.sem, pe.sem.value),)
                defer(2, windows)
                return u_did
            return run

        def l0_norm():
            run_due(everything=True)
            run_background(everything=True)
            did_all = tuple(conv_did[b] for b in range(8))
            slots, n_did = [], []
            for tt_ in range(NT):
                stats, mean_var = small_cols(12), small_cols(2)
                banks = []
                for h in range(2):
                    i, free = take_bank()
                    for b in range(4):
                        did = transpose(bank[i][:, b * P:(b + 1) * P], conv_out[:, 4 * h + b, tt_ * P:(tt_ + 1) * P],
                                        waits=did_all + free, last=b == 3)
                    banks.append(i)
                    stat_did = dve.op(lambda e, o=stats[:, 6 * h:6 * h + 6], s=bank[i]: e.bn_stats(o, s), (did,))
                aggr_did = dve.op(lambda e, o=mean_var, s=stats: e.bn_aggr(o, s), (stat_did,))
                rstd = small_cols(1)
                r_did = inv_sqrt(rstd, mean_var[:, 1:2], 1, (aggr_did,))
                s, free = take_z()
                slots.append(s)
                for h in range(2):
                    did = v_ts(z_flat[s][:, h * CH:(h + 1) * CH], bank[banks[h]], mean_var[:, 0:1], ALU.subtract,
                               rstd, ALU.mult, waits=(r_did,) + free)
                    bank_free[banks[h]] = (did,)
                n_did.append(did)
            work = conv_in_flat
            for j in range(2):
                group_ready[("B", 2 + j)] = ()

                def evacuate(half, view, done):
                    a = work[:, half * CH:(half + 1) * CH].rearrange("p (k t) -> p k t", k=2)
                    s = work[:, D // 2 + half * CH:D // 2 + (half + 1) * CH].rearrange("p (k t) -> p k t", k=2)
                    for k in range(2):
                        b = GK * j + 2 * half + k
                        g_, b_ = (par[:, ROWS[n] + b:ROWS[n] + b + 1] for n in ("ln_g", "ln_b"))
                        a_did = v_ts(a[:, k, :], view[:, k, :], g_, ALU.mult, b_, ALU.add,
                                     waits=(done,) + state.get(("silu", half), did_all))
                    for k in range(2):
                        b = GK * j + 2 * half + k
                        g_, b_ = (par[:, ROWS[n] + b:ROWS[n] + b + 1] for n in ("ln_g", "ln_b"))
                        s_did = a_affine(s[:, k, :], view[:, k, :], ACT.Sigmoid, g_, b_, (a_did,))
                    y_did = tt(dve, a, a, s, ALU.mult, (a_did, s_did))
                    state[("silu", half)] = store_halves(
                        "B", GK * (2 + j) + 2 * half, 2,
                        lambda hi, w: a_copy(hi, a, waits=w + (y_did,)),
                        lambda lo, hi, w: tt(dve, lo, a, hi, ALU.subtract, w))
                    return (a_did, s_did)
                to_features(lambda tt_: z_flat[slots[tt_]][:, j * CH:(j + 1) * CH], tuple(n_did), evacuate)
            for s in slots:
                z_free[s] = ((pe.sem, pe.sem.value),)
            state["conv_free"] = state[("silu", 0)] + state[("silu", 1)] + ((pe.sem, pe.sem.value),)

        w = t["ab_w_in"][0]
        for j in range(2):
            product(w, 0, 16, D_POOL + j * CH, "A", 0, l0_value,
                    (lambda: begin(ROWS["mix_pre0"], False)) if j == 0 else
                    (lambda: (load_pool_w(), per_step.__setitem__(0, 5.3))))
            product(w, 0, 16, D_POOL + D_CONV + j * CH, "A", 0, l0_gate(j))
        for j in range(2):
            product(w, 0, 16, j * CH, "A", 0, l0_pool(j))
        w = t["ab_w_out"][0]

        def l0_out_first(n):
            return lambda ps, done: add_block(n, True, ps, done)

        def finish(n, alone):
            return lambda ps, done: finish_block(n, ps, done, alone)

        for n in range(NG):
            product(w, 0, 8, n * CH, "B", 0, l0_out_first(n),
                    (lambda: (run_due(everything=True), load_gain(t["mix_post_g"][0]))) if n == 0 else None)
        for n in range(NG):
            product(w, D_POOL, 8, n * CH, "B", 2, finish(n, False), l0_norm if n == 0 else None)

        def mlp(layer):
            w1, w2 = t["ffn_w1"][layer], t["ffn_w2"][layer]
            n_blocks = D_FF // FF_BLOCK

            def hidden(group):
                def run(ps, done):
                    s, r_did = scaled(ps, done, ACT.Relu)
                    dids = tuple(tt(pool, z[:, s, tt_, :], z[:, s, tt_, :], z[:, s, tt_, :], ALU.mult, (r_did[tt_],))
                                 for tt_ in range(NT))

                    def turn():
                        to_features(lambda tt_: z[:, s, tt_, :], dids, split_plain("B", group))
                        z_free[s] = ((pe.sem, pe.sem.value),)
                    defer(2, turn)
                    return r_did
                return run

            def up(b):
                for j in range(2):
                    before = None
                    if (b, j) == (0, 0):
                        before = lambda: begin(ROWS[f"ffn_pre{layer}"], True)
                    elif (b, j) == (0, 1):
                        before = lambda: load_gain(t["ffn_post_g"][layer])
                    product(w1, 0, 16, b * FF_BLOCK + j * CH, "A", 0, hidden((2 * b + j) % NG), before)

            def down(b):
                for n in range(NG):
                    if b == n_blocks - 1:
                        done = finish(n, False)
                    else:
                        done = (lambda n: lambda ps, did: add_block(n, b == 0, ps, did))(n)
                    product(w2, b * FF_BLOCK, 8, n * CH, "B", (2 * b) % NG, done)

            up(0)
            for b in range(1, n_blocks):
                up(b)
                down(b - 1)
            down(n_blocks - 1)

        if stop != "mix0":
            mlp(0)

        short_in = conv_in_flat[:, 0:GK * (TOK + SHORT_K - 1)].rearrange("p (b t) -> p b t", b=GK)
        short_out = conv_out_flat[:, 0:GK * TOK].rearrange("p (b t) -> p b t", b=GK)
        SPAD = SHORT_K - 1

        def l1_start():
            begin(ROWS["mix_pre1"], True)
            state["spad"] = (pool.op(lambda e: e.memset(short_in[:, :, 0:SPAD], 0.0), state["conv_free"]),)
            state["short_free"] = ()
            state["y_free"] = ()

        def l1_c(ps, done):
            state["c"] = scaled(ps, done)
            return state["c"][1]

        def l1_u(j):
            def run(ps, done):
                c, c_did = state["c"]
                dids = tuple(v_stt(z[:, c, tt_, :], ps[tt_], rs[0][:, tt_:tt_ + 1], z[:, c, tt_, :], ALU.mult,
                                   ALU.mult, (done, c_did[tt_])) for tt_ in range(NT))

                def turn():
                    out = []

                    def evacuate(half, view, did):
                        out.append(a_copy(short_in[:, 2 * half:2 * half + 2, SPAD:], view,
                                          waits=(did,) + state["spad"] + state["short_free"]))
                        return out[-1:]
                    to_features(lambda tt_: z[:, c, tt_, :], dids, evacuate)
                    z_free[c] = ((pe.sem, pe.sem.value),)
                    did = None
                    for b in range(GK):
                        for k in range(SHORT_K):
                            col = COL_SHORT + k * (D // P) + GK * j + b
                            src, wk, o = short_in[:, b, k:k + TOK], par[:, col:col + 1], short_out[:, b, :]
                            if k == 0:
                                did = v_ts(o, src, wk, ALU.mult, waits=tuple(out) + state["y_free"])
                            else:
                                did = v_stt(o, src, wk, o, ALU.mult, ALU.add, (did,))
                    state["short_did"] = did
                    state["short_free"] = (did,)
                defer(2, turn)
                return dids
            return run

        def l1_b(j):
            def run(ps, done):
                b, b_did = scaled(ps, done)

                def turn():
                    group_ready[("B", j)] = ()
                    free = []

                    def evacuate(half, view, did):
                        y = short_out[:, 2 * half:2 * half + 2, :]
                        y_did = tt(dve, y, view, y, ALU.mult, (did, state["short_did"]))
                        free.extend(store_halves(
                            "B", GK * j + 2 * half, 2,
                            lambda hi, w: a_copy(hi, y, waits=w + (y_did,)),
                            lambda lo, hi, w: tt(dve, lo, y, hi, ALU.subtract, w)))
                        return (y_did,)
                    to_features(lambda tt_: z[:, b, tt_, :], b_did, evacuate)
                    z_free[b] = ((pe.sem, pe.sem.value),)
                    state["y_free"] = tuple(free)
                defer(2, turn)
                return b_did
            return run

        if stop not in ("mix0", "ffn0"):
            w = t["sc_w_in"][0]
            for j in range(NG):
                product(w, 0, 16, D + j * CH, "A", 0, l1_c,
                        l1_start if j == 0 else (lambda: load_gain(t["mix_post_g"][1])) if j == 1 else None)
                product(w, 0, 16, 2 * D + j * CH, "A", 0, l1_u(j))
                product(w, 0, 16, j * CH, "A", 0, l1_b(j))
            w = t["sc_w_out"][0]
            for n in range(NG):
                product(w, 0, 16, n * CH, "B", 0, finish(n, True))
            if stop != "mix1":
                mlp(1)

        W_ATT = HEADS * HD
        q_T = acc_flat[:, 0:HEADS * TOK].rearrange("p (h t) -> p h t", h=HEADS)
        k_T = acc_flat[:, HEADS * TOK:2 * HEADS * TOK].rearrange("p (h t) -> p h t", h=HEADS)
        v_tok = gain_row.rearrange("p (t c) -> p t c", t=NT)
        att = conv_out_flat.rearrange("p (t c) -> p t c", t=NT)
        vg = conv_in_flat[:, 0:NT * W_ATT].rearrange("p (t c) -> p t c", t=NT)
        ws_T = ws_flat.rearrange("p (g c) -> p g c", g=HEADS)
        merged = acc
        HPC = CH // HD

        def l2_start():
            begin(ROWS["pre2"], True)
            state["pt"] = []

        def l2_spatial():
            s, free = take_z()
            raw = z_flat[s].rearrange("p (g c) -> p g c", g=HEADS)
            did = sp.dma(raw, t["w_spatial_2"][0].rearrange("g t s -> t g s"), ws_loaded, free)
            did = pool.op(lambda e: e.affine_select(out=raw, in_=raw, compare_op=ALU.is_ge, fill=0.0, base=0,
                                                    pattern=[[0, HEADS], [-1, P]], channel_multiplier=1), (did, sgu_did))
            for h in range(2):
                i, bfree = take_bank()
                for g in range(4):
                    tr = transpose(bank[i][:, g * P:(g + 1) * P], raw[:, 4 * h + g, :], waits=(did,) + bfree, last=g == 3)
                ws_did = a_copy(ws_flat[:, h * CH:(h + 1) * CH], bank[i], waits=(tr,))
                bank_free[i] = (ws_did,)
            state["ws_did"] = ws_did
            z_free[s] = (tr,)

        def heads_norm(src, dids, waits_out=()):
            tmp, free = take_z()
            sums, factors = small_cols(NT * HPC), small_cols(NT * HPC)
            s_did = ()
            for tt_ in range(NT):
                sq = tt(pool, z[:, tmp, tt_, :], src[tt_], src[tt_], ALU.mult, (dids[tt_],) + free)
                s_did += (dve.op(lambda e, o=sums[:, tt_ * HPC:(tt_ + 1) * HPC], i=z[:, tmp, tt_, :].rearrange("p (h c) -> p h c", h=HPC):
                                 e.reduce_sum(o, i, axis=AXIS.X), (sq,)),)
            f_did = inv_sqrt(factors, sums, HD, s_did)
            out = ()
            for tt_ in range(NT):
                v3 = src[tt_].rearrange("p (h c) -> p h c", h=HPC)
                f3 = factors[:, tt_ * HPC:(tt_ + 1) * HPC].unsqueeze(2).to_broadcast([P, HPC, HD])
                out += (tt(dve, v3, v3, f3, ALU.mult, (f_did,)),)
            z_free[tmp] = s_did
            return out

        def l2_qk(dst, key, j):
            def run(ps, done):
                s, s_did = scaled(ps, done)
                n_did = heads_norm([z[:, s, tt_, :] for tt_ in range(NT)], s_did)
                gain = par[:, ROWS[key]:ROWS[key] + 1]

                def turn():
                    def evacuate(half, view, did):
                        h = HPC * j + 2 * half
                        state["qk_did"] = a_copy(dst[:, h:h + 2, :], view, gain, (did,) + acc_free[0])
                        return (state["qk_did"],)
                    to_features(lambda tt_: z[:, s, tt_, :], n_did, evacuate)
                    z_free[s] = ((pe.sem, pe.sem.value),)
                defer(3, turn)
                return s_did
            return run

        def l2_v(j):
            def run(ps, done):
                dids = tuple(a_copy(v_tok[:, tt_, j * CH:(j + 1) * CH], ps[tt_], rs[0][:, tt_:tt_ + 1],
                                    (done, rs_did[0]) + gain_read[0]) for tt_ in range(NT))
                state["v_did"] = dids
                return dids
            return run

        def silu_of(ps, done, out, waits=()):
            s_did = tuple(a_copy(out[tt_], ps[tt_], rs[0][:, tt_:tt_ + 1], (done, rs_did[0]) + tuple(waits), ACT.Sigmoid)
                          for tt_ in range(NT))
            return tuple(v_stt(out[tt_], ps[tt_], rs[0][:, tt_:tt_ + 1], out[tt_], ALU.mult, ALU.mult, (s_did[tt_],))
                         for tt_ in range(NT))

        def l2_za(j):
            def run(ps, done):
                dids = silu_of(ps, done, [att[:, tt_, j * CH:(j + 1) * CH] for tt_ in range(NT)], state["y_free"])
                state[("za", j)] = dids
                if j == 1:
                    defer(1, attention)
                return dids
            return run

        scores_buf = sbuf("scores", 2 * 3 * P)[:, :].rearrange("p (s c) -> p s c", s=2)
        probs_T = prod_buf.rearrange("p s t -> p (s t)")
        score_free = {0: (), 1: ()}
        probs_T_free = [()]
        head = {}

        def att_scores(h):
            i, free = take_bank()
            ps = bank[i]
            ready = (state["qk_did"], mask_did) + free
            mm(ps[:, 0:TOK], q_T[:, h, P:TOK], k_T[:, h, :], True, True, ready)
            did = mm_last(ps[:, TOK:3 * P], q_T[:, h, 0:P], k_T[:, h, 0:P], True, True)
            s = scores_buf[:, h % 2, :]
            m_did = tt(dve, s, ps[:, 0:3 * P], mask, ALU.add, (did,) + score_free[h % 2])
            bank_free[i] = (m_did,)
            top, bias, total, inv = small_cols(2), small_cols(2), small_cols(2), small_cols(2)
            parts = (s[:, TOK:3 * P], s[:, 0:TOK])
            t_did = tuple(dve.op(lambda e, o=top[:, n:n + 1], v=parts[n]: e.reduce_max(o, v, axis=AXIS.X), (m_did,))
                          for n in range(2))
            b_did = v_ts(bias, top, -SCALE, ALU.mult, waits=t_did)
            e_did = tuple(a_sum(parts[n], parts[n], ACT.Exp, total[:, n:n + 1], (b_did,), bias=bias[:, n:n + 1], scale=SCALE)
                          for n in range(2))
            i_did = dve.op(lambda e: e.reciprocal(inv, total), e_did)
            head[h] = (s, inv, e_did, i_did)

        def att_turn(h):
            s, inv, e_did, i_did = head[h]
            i, free = take_bank()
            for b in range(3):
                did = transpose(bank[i][:, b * P:(b + 1) * P], s[:, b * P:(b + 1) * P], waits=e_did + free, last=b == 2)
            score_free[h % 2] = (did,)
            c_did = a_copy(probs_T[:, 0:3 * P], bank[i][:, 0:3 * P], waits=(did,) + probs_T_free[0])
            bank_free[i] = (c_did,)
            head[h] += (c_did,)

        def att_values(h):
            s, inv, e_did, i_did, c_did = head[h]
            i, free = take_bank()
            cols = slice(h * HD, (h + 1) * HD)
            ready = (c_did,) + state["v_did"] + free
            mm(bank[i][:, 0:HD], probs_T[:, 2 * P:3 * P], v_tok[:, 0, cols], True, True, ready)
            mm(bank[i][:, HD:2 * HD], probs_T[:, 0:P], v_tok[:, 0, cols], True, False)
            did = mm_last(bank[i][:, HD:2 * HD], probs_T[:, P:2 * P], v_tok[:, 1, cols], False, True)
            probs_T_free[0] = (did,)
            o_did = tuple(v_stt(att[:, n, cols], bank[i][:, n * HD:(n + 1) * HD], inv[:, n:n + 1], att[:, n, cols],
                                ALU.mult, ALU.mult, (did, i_did) + state[("za", 0)] + state[("za", 1)]) for n in range(2))
            bank_free[i] = o_did
            state[("att", h)] = o_did

        def att_out(j):
            to_features(lambda tt_: att[:, tt_, j * CH:(j + 1) * CH],
                        sum((state[("att", h)] for h in range(HPC * j, HPC * (j + 1))), ()), split_plain("B", j))

        def attention():
            for h in range(HEADS + 1):
                if h < HEADS:
                    background.append(lambda h=h: att_scores(h))
                if h >= 1:
                    background.append(lambda h=h: att_turn(h - 1))
                    background.append(lambda h=h: att_values(h - 1))
            for j in range(2):
                background.append(lambda j=j: att_out(j))
            per_step[0] = 0.6

        def gelu_into(ps, done, out, tmp, waits):
            dids = ()
            for tt_ in range(NT):
                a = a_copy(out[tt_], ps[tt_], rs[0][:, tt_:tt_ + 1], (done, rs_did[0]) + tuple(waits))
                s = tt(pool, tmp[tt_], out[tt_], out[tt_], ALU.mult, (a,) + tuple(waits))
                s = v_ts(tmp[tt_], tmp[tt_], GELU_A, ALU.mult, 1.0, ALU.add, waits=(s,))
                s = tt(pool, tmp[tt_], tmp[tt_], out[tt_], ALU.mult, (s,))
                s = a_copy(tmp[tt_], tmp[tt_], float(GELU_B), (s,), ACT.Sigmoid)
                dids += (tt(pool, out[tt_], out[tt_], tmp[tt_], ALU.mult, (s,)),)
            return dids

        def l2_vb(j):
            def run(ps, done):
                tmp, free = take_z()
                out = [vg[:, tt_, j * CH:(j + 1) * CH] for tt_ in range(NT)]
                g_did = gelu_into(ps, done, out, [z[:, tmp, tt_, :] for tt_ in range(NT)],
                                  free + state["short_free"])
                z_free[tmp] = g_did
                n_did = heads_norm(out, g_did)
                row = sgu_row.unsqueeze(1).to_broadcast([P, HPC, HD])
                dids = ()
                for tt_ in range(NT):
                    v3 = out[tt_].rearrange("p (h c) -> p h c", h=HPC)
                    dids += (tt(pool, v3, v3, row, ALU.mult, (n_did[tt_], sgu_did)),)
                state[("vg", j)] = dids
                return g_did
            return run

        def l2_ub(j):
            def run(ps, done):
                u, u_free = take_z()
                tmp, free = take_z()
                out = [z[:, u, tt_, :] for tt_ in range(NT)]
                g_did = gelu_into(ps, done, out, [z[:, tmp, tt_, :] for tt_ in range(NT)], free + u_free)
                z_free[tmp] = g_did

                def mix():
                    dids = ()
                    for tt_ in range(NT):
                        i, bfree = take_bank()
                        for c in range(HPC):
                            g = HPC * j + c
                            did = mm_last(bank[i][:, c * HD:(c + 1) * HD], ws_T[:, g, :], vg[:, tt_, g * HD:(g + 1) * HD],
                                          True, True, (state["ws_did"], state[("vg", j)][tt_]) + bfree)
                        for c in range(HPC):
                            g = HPC * j + c
                            o = z[:, u, tt_, c * HD:(c + 1) * HD]
                            last = v_stt(o, bank[i][:, c * HD:(c + 1) * HD],
                                         par[:, ROWS["b_spatial"] + g:ROWS["b_spatial"] + g + 1], o,
                                         ALU.add, ALU.mult, (did, g_did[tt_]))
                        bank_free[i] = (last,)
                        dids += (last,)
                    state["sgu"] = (u, dids)
                defer(3, mix)
                return (g_did[0], g_did[1])
            return run

        def l2_zb(j):
            def run(ps, done):
                tmp, free = take_z()
                zz = [z[:, tmp, tt_, :] for tt_ in range(NT)]
                s_did = silu_of(ps, done, zz, free)
                u, u_did = state["sgu"]
                dids = tuple(tt(pool, z[:, u, tt_, :], z[:, u, tt_, :], zz[tt_], ALU.mult, (u_did[tt_], s_did[tt_]))
                             for tt_ in range(NT))
                z_free[tmp] = dids

                def turn():
                    to_features(lambda tt_: z[:, u, tt_, :], dids, split_plain("B", 2 + j))
                    z_free[u] = ((pe.sem, pe.sem.value),)
                defer(2, turn)
                return s_did
            return run

        def l2_gate(key):
            def run(ps, done):
                state[key] = scaled(ps, done, ACT.Sigmoid)
                return state[key][1]
            return run

        def l2_proj(n, key):
            def run(ps, done):
                g, g_did = state[key]
                cols = slice(n * CH, (n + 1) * CH)
                dids = ()
                for tt_ in range(NT):
                    out = merged[:, tt_, cols]
                    if key == "ga":
                        did = tt(dve, out, ps[tt_], z[:, g, tt_, :], ALU.mult,
                                 (done, g_did[tt_], state["qk_read"]))
                        state[("m", n, tt_)] = did
                        dids += (did,)
                    else:
                        did = tt(dve, z[:, g, tt_, :], ps[tt_], z[:, g, tt_, :], ALU.mult, (done, g_did[tt_]))
                        dids += (did,)
                        state[("m", n, tt_)] = tt(pool, out, out, z[:, g, tt_, :], ALU.add, (did, state[("m", n, tt_)]))
                z_free[g] = dids if key == "ga" else (state[("m", n, 0)], state[("m", n, 1)])
                if key == "gb" and n == NG - 1:
                    for g_ in range(NG):
                        to_features(lambda tt_: merged[:, tt_, g_ * CH:(g_ + 1) * CH],
                                    (state[("m", g_, 0)], state[("m", g_, 1)]), split_plain("A", g_))
                return dids
            return run

        def before_proj():
            run_due(everything=True)
            run_background(everything=True)
            state["qk_read"] = (pe.sem, pe.sem.value)

        out_dram = t["out"].rearrange("b (t p) d -> p (b t) d", p=P)

        def l2_out(n):
            def run(ps, done):
                cols = slice(n * CH, (n + 1) * CH)
                dids = ()
                for tt_ in range(NT):
                    did = tt(dve, x[:, tt_, cols], ps[tt_], x[:, tt_, cols], ALU.add, (done,) + x_ready[(n, tt_)])
                    sp.dma(out_dram[:, tt_, cols], x[:, tt_, cols], out_written, (did,))
                    dids += (did,)
                return dids
            return run

        if stop is None:
            w = t["w_in_2"][0]

            def cols_of(part, j):
                return part * W_ATT + j * CH

            GA, GB = 7 * W_ATT, 7 * W_ATT + D
            for j in range(2):
                product(w, 0, 16, cols_of(0, j), "A", 0, l2_qk(q_T, "q_g", j), l2_start if j == 0 else l2_spatial)
            for j in range(2):
                product(w, 0, 16, cols_of(1, j), "A", 0, l2_qk(k_T, "k_g", j))
            for j in range(2):
                product(w, 0, 16, cols_of(2, j), "A", 0, l2_v(j))
            for j in range(2):
                product(w, 0, 16, cols_of(3, j), "A", 0, l2_za(j))
            for j in range(2):
                product(w, 0, 16, cols_of(5, j), "A", 0, l2_vb(j))
            for j in range(2):
                product(w, 0, 16, cols_of(4, j), "A", 0, l2_ub(j))
                product(w, 0, 16, cols_of(6, j), "A", 0, l2_zb(j))
            for n in range(NG):
                product(w, 0, 16, GA + n * CH, "A", 0, l2_gate("ga"), before_proj if n == 0 else None)
                product(w, 0, 16, GB + n * CH, "A", 0, l2_gate("gb"))
                product(t["w_proj_a_2"][0], 0, 8, n * CH, "B", 0, l2_proj(n, "ga"))
                product(t["w_proj_b_2"][0], 0, 8, n * CH, "B", 2, l2_proj(n, "gb"))
            for n in range(NG):
                product(t["w_out_2"][0], 0, 16, n * CH, "A", 0, l2_out(n))

        steps = [(c, i) for c in chunks for i in range(c["nk"] // STEP_K)]
        STEPS_PER_LOAD = GK // STEP_K
        loads = len(steps) // STEPS_PER_LOAD
        next_load = [0]

        def load_weights(n):
            c, i = steps[n * STEPS_PER_LOAD]
            row = c["row0"] + i * STEP_K * P
            src = c["w"][row:row + GK * P, c["col0"]:c["col0"] + CH].rearrange("(k p) c -> p k c", p=P)
            slot = n % RAW_SLOTS
            used = ((lo_made, STEPS_PER_LOAD * (n - RAW_SLOTS + 1)),) if n >= RAW_SLOTS else ()
            sp.dma(w_raw[:, slot, :].rearrange("p (k c) -> p k c", k=GK), src, raw_loaded[slot], used)

        def split_weights(s):
            n, part = divmod(s, STEPS_PER_LOAD)
            while next_load[0] < loads and next_load[0] <= n + RAW_SLOTS - 1:
                load_weights(next_load[0])
                next_load[0] += 1
            raw = w_raw[:, n % RAW_SLOTS, part * STEP_K * CH:(part + 1) * STEP_K * CH]
            loaded = (raw_loaded[n % RAW_SLOTS], 16 * (n // RAW_SLOTS + 1))
            free = (step_done, s - SPLIT_SLOTS + 1) if s >= SPLIT_SLOTS else None
            slot = s % SPLIT_SLOTS
            hi = a_copy(w_hi[:, slot, :], raw, waits=(loaded, free), sem=hi_made)
            tt(dve, w_lo[:, slot, :], raw, w_hi[:, slot, :].bitcast(F32), ALU.subtract, (hi, free), sem=lo_made)

        pair_free = [(), ()]
        for s in range(min(AHEAD, len(steps))):
            split_weights(s)
        pair = -1
        for s, (c, i) in enumerate(steps):
            now[0] = s
            if i == 0:
                pair += 1
                if c["before"]:
                    c["before"]()
            if s + AHEAD < len(steps):
                split_weights(s + AHEAD)
            ps = [bank[2 * (pair % 2) + tt_] for tt_ in range(NT)]
            group = c["group0"] + i * STEP_K // GK
            hi, lo = halves[c["buf"]]
            pe.wait((lo_made, s + 1), *group_ready[(c["buf"], group)])
            if i == 0:
                pe.wait(*pair_free[pair % 2])
            slot = s % SPLIT_SLOTS
            last_i = i == c["nk"] // STEP_K - 1
            for k in range(STEP_K):
                kt = GK * c["group0"] + i * STEP_K + k
                wh, wl = (v[:, slot, k * CH:(k + 1) * CH] for v in (w_hi, w_lo))
                for tt_ in range(NT):
                    tok = slice(tt_ * P, (tt_ + 1) * P)
                    first, last = i == 0 and k == 0, last_i and k == STEP_K - 1
                    mm(ps[tt_], lo[:, kt, tok], wh, first, False)
                    mm(ps[tt_], hi[:, kt, tok], wl, False, False)
                    if k == STEP_K - 1 and tt_ == NT - 1:
                        done = mm_last(ps[tt_], hi[:, kt, tok], wh, False, last, sem=step_done)
                    else:
                        mm(ps[tt_], hi[:, kt, tok], wh, False, last)
            group_read[(c["buf"], group)] = done
            if last_i:
                pair_free[pair % 2] = tuple(c["done"](ps, done))
            run_due()
            run_background()
        run_due(everything=True)
        if stop is not None:
            sp.wait(sgu_did)
            begin(ROWS["mix_pre0"], True)
            run_due(everything=True)
            for g in range(NG):
                for tt_ in range(NT):
                    cols = slice(g * CH, (g + 1) * CH)
                    sp.dma(out_dram[:, tt_, cols], x[:, tt_, cols], out_written, x_ready[(g, tt_)])
        sp.wait((out_written, out_written.value))

        block = ctx.enter_context(nc.Block())

        @block.sync
        def _(e):
            sp.replay(e)

        @block.scalar
        def _(e):
            act.replay(e)

        @block.vector
        def _(e):
            dve.replay(e)

        @block.gpsimd
        def _(e):
            pool.replay(e)

        @block.tensor
        def _(e):
            pe.replay(e)


INPUTS = ("x", "mix_pre_g", "mix_post_g", "ffn_pre_g", "ffn_post_g", "ab_w_in", "pool_w", "pool_scale", "conv_w",
          "conv_b", "conv_ln_g", "conv_ln_b", "ab_w_out", "sc_w_in", "sc_conv_w", "sc_w_out", "ffn_w1", "ffn_w2",
          "norm_g_2", "w_in_2", "q_norm_g_2", "k_norm_g_2", "sgu_norm_g_2", "w_spatial_2", "b_spatial_2",
          "w_proj_a_2", "w_proj_b_2", "w_out_2")


def kernel(**inputs):
    import concourse.bacc as bacc
    from concourse.bass_utils import run_bass_kernel_spmd

    nc = bacc.Bacc("TRN2", target_bir_lowering=False, num_devices=1)
    arrays, aps = {}, {}
    for name in INPUTS:
        a = np.ascontiguousarray(inputs[name])
        arrays[f"in_{name}"] = a
        aps[name] = nc.dram_tensor(f"in_{name}", a.shape, mybir.dt.from_np(a.dtype), kind="ExternalInput").ap()
    aps["out"] = nc.dram_tensor("out_x", (1, TOK, D), F32, kind="ExternalOutput").ap()
    build(nc, aps)
    r = run_bass_kernel_spmd(nc, [arrays], core_ids=[0])
    return r.results[0]["out_x"]
```

```python
import numpy as np
import concourse.bass as bass
from concourse import mybir
from concourse.alu_op_type import AluOpType as ALU
from contextlib import ExitStack

F32 = mybir.dt.float32
F32R = mybir.dt.float32r
ACT = mybir.ActivationFunctionType
AXIS = mybir.AxisListType

P = 128
TOK = 256
NT = TOK // P
D = 2048
CH = 512
GK = CH // P
NG = D // CH
EPS = 1e-6
D_POOL = 1024
D_CONV = 1024
CONV_K = 31
SHORT_K = 3
D_FF = 4 * D
FF_BLOCK = 1024
WINDOWS = (2, 4, 8, 16)
HEADS = 8
HD = 128
SCALE = float(HD) ** -0.5
GELU_A = 0.044715
GELU_B = 2.0 * (2.0 / np.pi) ** 0.5

RAW_SLOTS = 3
SPLIT_SLOTS = 4
CONV_PER_STEP = 6.0
AHEAD = SPLIT_SLOTS - 1
HELD_AHEAD = 1
STEP_K = 2

ROWS = {}
_at = 0
for _name, _n in (("mix_pre0", 16), ("mix_pre1", 16), ("ffn_pre0", 16), ("ffn_pre1", 16), ("pre2", 16),
                  ("pool_scale", 8), ("conv_b", 8), ("ln_g", 8), ("ln_b", 8), ("b_spatial", 8),
                  ("q_g", 1), ("k_g", 1)):
    ROWS[_name] = _at
    _at += _n
N_ROWS = _at
CONV_ROWS = CONV_K * D_CONV // P // 2
SHORT_ROWS = SHORT_K * D // P
COL_CONV = N_ROWS
COL_SHORT = COL_CONV + 2 * CONV_ROWS
FIRST_COL = COL_SHORT + SHORT_ROWS
N_PAR = FIRST_COL + 16


class Queue:

    def __init__(self, sem):
        self.todo, self.sem, self.seen = [], sem, {}

    def wait(self, *tokens):
        for token in tokens:
            if token is None:
                continue
            sem, value = token
            if self.seen.get(sem.name, 0) < value:
                self.seen[sem.name] = value
                self.todo.append((lambda e, s=sem.sem, v=value: e.wait_ge(s, v)))

    def op(self, emit, waits=(), sem=None):
        self.wait(*waits)
        sem = sem or self.sem
        sem.value += 1
        self.todo.append(lambda e: emit(e).then_inc(sem.sem, 1))
        return (sem, sem.value)

    def quiet(self, emit, waits=()):
        self.wait(*waits)
        self.todo.append(emit)

    def dma(self, out, in_, sem, waits=()):
        self.wait(*waits)
        sem.value += 16
        self.todo.append(lambda e: e.dma_start(out, in_).then_inc(sem.sem, 16))
        return (sem, sem.value)

    def replay(self, e):
        for emit in self.todo:
            emit(e)


class Counter:

    def __init__(self, name, sem):
        self.name, self.sem, self.value = name, sem, 0


def build(nc, t):
    ctx = ExitStack()
    with ctx:
        def sbuf(name, cols, dt=F32):
            return ctx.enter_context(nc.sbuf_tensor(name, [P, cols], dt))

        def counter(name):
            return Counter(name, ctx.enter_context(nc.semaphore(name)))

        x = sbuf("x_res", NT * D)[:, :].rearrange("p (t d) -> p t d", t=NT)
        acc_flat = sbuf("acc", NT * D)[:, :]
        acc = acc_flat.rearrange("p (t d) -> p t d", t=NT)
        gain_row = sbuf("gain_row", D)[:, :]
        conv_in_flat = sbuf("conv_in", 8 * (TOK + CONV_K - 1))[:, :]
        conv_out_flat = sbuf("conv_out", 8 * TOK)[:, :]
        par = sbuf("par", N_PAR)[:, :]
        ident = sbuf("ident", P)[:, :]
        mask = sbuf("mask", 3 * P)[:, :]
        ws_flat = sbuf("ws_T", HEADS * HD)[:, :]
        sgu_row = sbuf("sgu_row", HD)[:, :]
        small = sbuf("small", 512)[:, :]
        neg_half = sbuf("neg_half", 16)[:, :]
        Z_SLOTS = 3
        z = sbuf("z", Z_SLOTS * NT * CH)[:, :].rearrange("p (s t c) -> p s t c", s=Z_SLOTS, t=NT)
        prod_rows = sbuf("tap_product", 2 * TOK)[:, :]
        scores_flat = sbuf("scores", 2 * 3 * P)[:, :]
        halves = {}
        for name in ("A", "B"):
            halves[name] = tuple(sbuf(f"{name}_{h}", D // P * TOK, F32R)[:, :].rearrange(
                "p (k t) -> p k t", t=TOK) for h in ("hi", "lo"))
        w_raw = sbuf("w_raw", RAW_SLOTS * GK * CH)[:, :].rearrange("p (s c) -> p s c", s=RAW_SLOTS)
        w_hi = sbuf("w_hi", SPLIT_SLOTS * STEP_K * CH, F32R)[:, :].rearrange("p (s c) -> p s c", s=SPLIT_SLOTS)
        w_lo = sbuf("w_lo", SPLIT_SLOTS * STEP_K * CH, F32R)[:, :].rearrange("p (s c) -> p s c", s=SPLIT_SLOTS)
        bank = [ctx.enter_context(nc.psum_tensor(f"bank{i}", [P, CH], F32))[:, :] for i in range(8)]

        raw_loaded = [counter(f"raw_loaded{i}") for i in range(RAW_SLOTS)]
        hi_made, lo_made = counter("hi_made"), counter("lo_made")
        step_done = counter("step_done")
        x_loaded = [counter(f"x_loaded{i}") for i in range(NG)]
        par_loaded = counter("par_loaded")
        first_loaded = counter("first_loaded")
        pool_w_loaded = counter("pool_w_loaded")
        gain_loaded = counter("gain_loaded")
        ws_loaded = counter("ws_loaded")
        sgu_loaded = counter("sgu_loaded")
        out_written = counter("out_written")
        pe = Queue(counter("pe_did"))
        act = Queue(counter("act_did"))
        dve = Queue(counter("dve_did"))
        pool = Queue(counter("pool_did"))
        sp = Queue(counter("sp_did"))

        def a_copy(out, in_, scale=1.0, waits=(), func=ACT.Copy, sem=None):
            return act.op(lambda e: e.activation(out, in_, func, scale=scale), waits, sem)

        def a_affine(out, in_, func, scale, bias, waits=()):
            return act.op(lambda e: e.activation(out, in_, func, scale=scale, bias=bias), waits)

        def a_sum(out, in_, func, accum, waits=(), **kw):
            return act.op(lambda e: e.activation(out, in_, func, accum_out=accum, **kw), waits)

        def tt(q, out, a, b, op, waits=(), sem=None):
            return q.op(lambda e: e.tensor_tensor(out, a, b, op), waits, sem)

        def v_ts(out, a, s1, op0, s2=None, op1=None, waits=()):
            if op1 is None:
                return dve.op(lambda e: e.tensor_scalar(out, a, s1, None, op0), waits)
            return dve.op(lambda e: e.tensor_scalar(out, a, s1, s2, op0, op1), waits)

        def v_stt(out, a, s, b, op0, op1, waits=()):
            return dve.op(lambda e: e.scalar_tensor_tensor(out, a, s, b, op0, op1), waits)

        def mm(out, lhsT, rhs, start, stop, waits=()):
            pe.quiet(lambda e: e.matmul(out, lhsT, rhs, start=start, stop=stop), waits)

        def mm_last(out, lhsT, rhs, start, stop, waits=(), sem=None):
            return pe.op(lambda e: e.matmul(out, lhsT, rhs, start=start, stop=stop), waits, sem)

        def transpose(out, in_, n=P, waits=(), last=False):
            emit = lambda e: e.transpose(out, in_, ident[0:n, 0:n])
            if last:
                return pe.op(emit, waits)
            return pe.quiet(emit, waits)

        small_at = [0]

        def small_cols(n):
            at = small_at[0]
            small_at[0] += n
            assert small_at[0] <= 512
            return small[:, at:at + n]

        def inv_sqrt(out, in_, n, waits):
            w = in_.shape[-1]
            mean = small_cols(w)
            did = v_ts(mean, in_, 1.0 / n, ALU.mult, EPS, ALU.add, waits=waits)
            return tt(pool, out, mean, neg_half[:, 0:w], ALU.pow, (did,))

        bank_free = {i: () for i in range(4, 8)}
        bank_at = [0]

        def take_bank():
            i = 4 + bank_at[0] % 4
            bank_at[0] += 1
            free, bank_free[i] = bank_free[i], None
            assert free is not None, "a bank's readers are queued before it is taken again"
            return i, free

        z_free = {i: () for i in range(Z_SLOTS)}
        z_at = [0]

        def take_z():
            i = z_at[0] % Z_SLOTS
            z_at[0] += 1
            free, z_free[i] = z_free[i], None
            assert free is not None, "a slot's readers are queued before it is taken again"
            return i, free

        group_ready = {(b, g): () for b in "AB" for g in range(NG)}
        group_read = {(b, g): None for b in "AB" for g in range(NG)}

        def store_halves(buf, k, n, hi_from, lo_from):
            hi, lo = (h[:, k:k + n, :] for h in halves[buf])
            read = group_read[(buf, k // GK)]
            hi_did = hi_from(hi, (read,))
            lo_did = lo_from(lo, hi.bitcast(F32), (read, hi_did))
            group_ready[(buf, k // GK)] += (hi_did, lo_did)
            return hi_did, lo_did

        def store_scaled(buf, k, view, gains, done):
            read = group_read[(buf, k // GK)]
            hi, lo = halves[buf]
            for n in range(2):
                hi_did = a_copy(hi[:, k + n, :], view[:, n, :], gains[n], (read, done))
            for n in range(2):
                lo_did = v_stt(lo[:, k + n, :], view[:, n, :], gains[n], hi[:, k + n, :].bitcast(F32),
                               ALU.mult, ALU.subtract, (hi_did,))
            group_ready[(buf, k // GK)] += (hi_did, lo_did)
            return hi_did, lo_did

        def to_features(src, waits, evacuate):
            for half in range(2):
                i, free = take_bank()
                view = bank[i].rearrange("p (k t) -> p k t", k=2)
                did = None
                for k in range(2):
                    for tt_ in range(NT):
                        f = (2 * half + k) * P
                        did = transpose(view[:, k, tt_ * P:(tt_ + 1) * P], src(tt_)[:, f:f + P],
                                        waits=tuple(waits) + tuple(free), last=(k, tt_) == (1, NT - 1))
                bank_free[i] = tuple(evacuate(half, view, did))

        def split_plain(buf, group):
            group_ready[(buf, group)] = ()

            def evacuate(half, view, done):
                return store_halves(
                    buf, GK * group + 2 * half, 2,
                    lambda hi, w: a_copy(hi, view, waits=w + (done,)),
                    lambda lo, hi, w: tt(dve, lo, view, hi, ALU.subtract, w))
            return evacuate

        chunks = []

        def product(w, row0, nk, col0, buf, group0, done, before=None, by_token=False):
            chunks.append(dict(w=w, row0=row0, nk=nk, col0=col0, buf=buf, group0=group0, done=done,
                               before=before, by_token=by_token))

        later = []
        background = []
        per_step = [1]
        now = [0]

        def defer(steps, fn):
            later.append((now[0] + steps, len(later), fn))

        def run_due(everything=False):
            while True:
                due = sorted((d for d in later if everything or d[0] <= now[0]), key=lambda d: d[:2])
                if not due:
                    return
                later.remove(due[0])
                due[0][2]()

        def run_background(everything=False):
            n = len(background) if everything else min(int(per_step[0] * (now[0] + 1)) - int(per_step[0] * now[0]), len(background))
            for _ in range(n):
                background.pop(0)()

        x_ready = {(g, tt_): () for g in range(NG) for tt_ in range(NT)}
        rs = [None]
        rs_did = [None]
        post = {}

        def settle(tt_):
            total, factor = small_cols(1), small_cols(1)
            parts = post["sums"][:, tt_, :]
            did = dve.op(lambda e: e.reduce_sum(total, parts, axis=AXIS.X), post["sum_did", tt_])
            post["factor", tt_] = factor, inv_sqrt(factor, total, D, (did,))

        def update(g, tt_):
            cols = slice(g * CH, (g + 1) * CH)
            factor, factor_did = post["factor", tt_]
            x_ready[(g, tt_)] = (v_stt(x[:, tt_, cols], acc[:, tt_, cols], factor, x[:, tt_, cols], ALU.mult, ALU.add,
                                       (factor_did, post["gained", g, tt_])),)

        def begin(gain_col, first=None):
            run_due(everything=True)
            run_background(everything=True)

            def turn(g):
                cols = slice(g * CH, (g + 1) * CH)
                group_ready[("A", g)] = ()

                def evacuate(half, view, done):
                    kt = GK * g + 2 * half
                    gains = [par[:, gain_col + kt + k:gain_col + kt + k + 1] for k in range(2)]
                    return store_scaled("A", kt, view, gains, done)
                to_features(lambda tt_: x[:, tt_, cols],
                            x_ready[(g, 0)] + x_ready[(g, 1)] + (par_did[0],), evacuate)

            def statistics():
                sums, factors = small_cols(NT), small_cols(NT)
                dids = ()
                for tt_ in range(NT):
                    waits = sum((x_ready[(g, tt_)] for g in range(NG)), ())
                    dids += (a_sum(acc[:, tt_, :], x[:, tt_, :], ACT.Square, sums[:, tt_:tt_ + 1], waits + acc_free[0]),)
                rs[0] = factors
                rs_did[0] = inv_sqrt(factors, sums, D, dids)
                acc_free[0] = dids

            if first:
                turn(0)
                first()
                for g in range(1, NG):
                    defer(2 * g - 2, lambda g=g: turn(g))
                defer(2 * NG - 2, statistics)
                return
            for g in range(NG):
                update(g, 1)
                if g in (1, 2):
                    turn(g - 1)
            defer(0, lambda: turn(2))
            defer(2, lambda: turn(3))
            defer(3, statistics)

        acc_free = [()]

        def add_block(n, first, ps, done):
            dids = ()
            for tt_ in range(NT):
                out = acc[:, tt_, n * CH:(n + 1) * CH]
                if first:
                    did = a_copy(out, ps[tt_], waits=(done,) + acc_free[0])
                else:
                    did = tt(dve, out, ps[tt_], out, ALU.add, (done,) + acc_did[(n, tt_)])
                acc_did[(n, tt_)] = (did,)
                dids += (did,)
            return dids

        acc_did = {}

        def finish_block(n, ps, done, alone, tiles):
            if n == 0:
                post["sums"] = small_cols(NT * NG).rearrange("p (t n) -> p t n", t=NT)
                post["sum_did", 0] = post["sum_did", 1] = ()
            dids = ()
            for tt_ in tiles:
                out = acc[:, tt_, n * CH:(n + 1) * CH]
                if alone:
                    did = dve.op(lambda e, o=out, i=ps[tt_]: e.tensor_copy(o, i), (done,) + acc_free[0])
                else:
                    did = tt(dve, out, ps[tt_], out, ALU.add, (done,) + acc_did[(n, tt_)])
                sq = a_sum(ps[tt_], out, ACT.Square, post["sums"][:, tt_, n:n + 1], (did,))
                post["sum_did", tt_] += (sq,)
                dids += (sq,)
            for tt_, did in zip(tiles, dids):
                if n == NG - 1:
                    settle(tt_)
                out = acc[:, tt_, n * CH:(n + 1) * CH]
                gained = tt(pool, out, out, gain_row[:, n * CH:(n + 1) * CH], ALU.mult, (did, gain_did[0]))
                post["gained", n, tt_] = gained
                gain_read[0] = (gained,)
            if n == NG - 1 and tiles == (0,):
                for g in range(NG):
                    update(g, 0)
            return dids

        gain_did, gain_read = [None], [()]

        def load_gain(src):
            gain_did[0] = sp.dma(gain_row, src.unsqueeze(0).to_broadcast([P, D]), gain_loaded, gain_read[0])

        par_did, rows_did, sgu_did = [None], [None], [None]
        z_flat = [z[:, s, :, :].rearrange("p t c -> p (t c)") for s in range(Z_SLOTS)]
        rows = z_flat[0]
        z_free[0] = None
        did = pool.op(lambda e: e.memset(ident, 0.0))
        ident_did = pool.op(lambda e: e.affine_select(out=ident, in_=ident, compare_op=ALU.not_equal, fill=1.0, base=0,
                                                      pattern=[[-1, P]], channel_multiplier=1), (did,))
        half_did = pool.op(lambda e: e.memset(neg_half, -0.5))
        pool.wait(half_did)

        first_rows = prod_rows[0:16, 0:P]
        x_dram = t["x"].rearrange("b (t p) d -> p (b t) d", p=P)

        def load_x(g):
            did = sp.dma(x[:, :, g * CH:(g + 1) * CH], x_dram[:, :, g * CH:(g + 1) * CH], x_loaded[g])
            for tt_ in range(NT):
                x_ready[(g, tt_)] = (did,)

        def load_first_gain():
            return sp.dma(first_rows, t["mix_pre_g"][0:1, :].rearrange("l (k p) -> (l k) p", p=P), first_loaded)

        def load_rows():
            sp.dma(rows[0:32, 0:P], t["mix_pre_g"].rearrange("l (k p) -> (l k) p", p=P), par_loaded)
            sp.dma(rows[32:64, 0:P], t["ffn_pre_g"].rearrange("l (k p) -> (l k) p", p=P), par_loaded)
            for name, key in (("norm_g_2", "pre2"), ("pool_scale", "pool_scale"), ("conv_b", "conv_b"),
                              ("conv_ln_g", "ln_g"), ("conv_ln_b", "ln_b"), ("q_norm_g_2", "q_g"),
                              ("k_norm_g_2", "k_g")):
                n = t[name].shape[1] // P
                sp.dma(rows[ROWS[key]:ROWS[key] + n, 0:P], t[name].rearrange("l (k p) -> (l k) p", p=P), par_loaded)
            sp.dma(rows[ROWS["b_spatial"]:ROWS["b_spatial"] + 8, 0:P], t["b_spatial_2"][0, :, :], par_loaded)
            taps = t["conv_w"].rearrange("l k (b p) -> (l k b) p", p=P)
            for h in range(2):
                sp.dma(rows[0:CONV_ROWS, (1 + h) * P:(2 + h) * P], taps[h * CONV_ROWS:(h + 1) * CONV_ROWS, :], par_loaded)
            return sp.dma(rows[0:SHORT_ROWS, 3 * P:4 * P], t["sc_conv_w"].rearrange("l k (b p) -> (l k b) p", p=P), par_loaded)

        def turn_first_gain(loaded):
            i, free = take_bank()
            did = transpose(bank[i][:, 0:16], first_rows, 16, (ident_did, loaded), last=True)
            bank_free[i] = (a_copy(par[:, FIRST_COL:FIRST_COL + 16], bank[i][:, 0:16], waits=(did,)),)
            par_did[0] = bank_free[i][0]

        def turn_rows(loaded):
            i, free = take_bank()
            blocks = (N_ROWS, CONV_ROWS, CONV_ROWS, SHORT_ROWS)
            for b, n in enumerate(blocks):
                did = transpose(bank[i][:, b * P:b * P + n], rows[0:n, b * P:(b + 1) * P], n,
                                (loaded,) + free, last=b == 3)
            col, dids = 0, ()
            for b, n in enumerate(blocks):
                dids += (a_copy(par[:, col:col + n], bank[i][:, b * P:b * P + n], waits=(did,)),)
                col += n
            par_did[0] = dids[-1]
            bank_free[i] = dids
            z_free[0] = (did,)
            dve.wait(par_did[0])

        did = pool.op(lambda e: e.memset(mask, 0.0))
        mask_did = did
        for c0 in (P, 2 * P):
            mask_did = pool.op(lambda e, v=mask[:, c0:c0 + P]: e.affine_select(
                out=v, in_=v, compare_op=ALU.is_ge, fill=-1e30, base=0, pattern=[[-1, P]], channel_multiplier=1), (did,))

        conv_in = conv_in_flat.rearrange("p (b t) -> p b t", b=8)
        conv_out = conv_out_flat.rearrange("p (b t) -> p b t", b=8)
        PAD = CONV_K - 1
        pad_did = pool.op(lambda e: e.memset(conv_in[:, :, 0:PAD], 0.0))

        band0 = gain_row[:, 0:4 * TOK].rearrange("p (g t) -> p g t", g=4)
        band1 = gain_row[:, 4 * TOK:4 * TOK + 4 * P].rearrange("p (g t) -> p g t", g=4)
        band_did = ()
        for g, w in enumerate(WINDOWS):
            for band, width, edge in ((band0[:, g, :], TOK, True), (band1[:, g, :], P, False)):
                did = pool.op(lambda e, v=band, c=1.0 / w: e.memset(v, c))
                if edge:
                    for tok in range(w - 1):
                        did = pool.op(lambda e, v=band[:, tok:tok + 1], c=1.0 / (tok + 1): e.memset(v, c), (did,))
                did = pool.op(lambda e, v=band, n=width: e.affine_select(
                    out=v, in_=v, compare_op=ALU.is_ge, fill=0.0, base=0, pattern=[[1, n]], channel_multiplier=-1), (did,))
                did = pool.op(lambda e, v=band, n=width, b=w - 1: e.affine_select(
                    out=v, in_=v, compare_op=ALU.is_ge, fill=0.0, base=b, pattern=[[-1, n]], channel_multiplier=1), (did,))
                band_did += (tt(pool, band[:, 0:P], band[:, 0:P], ident, ALU.subtract, (did,)),)

        pool_w = acc_flat[:, 0:D].rearrange("p (g c e) -> p g c e", g=4, c=2)
        pool_w_did = []

        def load_pool_w():
            pool_w_did.append(sp.dma(pool_w, t["pool_w"].rearrange("l g (c p) e -> p (l g) c e", p=P),
                                     pool_w_loaded, acc_free[0]))

        state = {}

        def scaled(ps, done, func=ACT.Copy):
            s, free = take_z()
            dids = tuple(a_copy(z[:, s, tt_, :], ps[tt_], rs[0][:, tt_:tt_ + 1], (done, rs_did[0]) + free, func)
                         for tt_ in range(NT))
            return s, dids

        def l0_value(ps, done):
            state["v"] = scaled(ps, done)
            return state["v"][1]

        def l0_gate(j):
            def run(ps, done):
                v, v_did = state["v"]
                g, g_did = scaled(ps, done, ACT.Sigmoid)
                dids = tuple(tt(pool, z[:, v, tt_, :], z[:, v, tt_, :], z[:, g, tt_, :], ALU.mult,
                                (v_did[tt_], g_did[tt_])) for tt_ in range(NT))
                z_free[g] = dids

                def turn():
                    out = []

                    def evacuate(half, view, did):
                        b = GK * j + 2 * half
                        out.append(a_copy(conv_in[:, b:b + 2, PAD:], view, waits=(did, pad_did)))
                        return out[-1:]
                    to_features(lambda tt_: z[:, v, tt_, :], dids, evacuate)
                    z_free[v] = (pe.sem, pe.sem.value),
                    convolve(GK * j, tuple(out))
                    if j == 1:
                        background.append(lambda: defer(1, lambda: l0_norm_tile(0)))
                defer(2, turn)
                return g_did
            return run

        def split_first():
            split_until(STEPS_PER_LOAD - 1)

        conv_did = {}
        V_BLOCKS = (0, 1, 4, 5)
        tap_at = [0]
        tap_slots = [prod_rows[:, n * TOK:(n + 1) * TOK] for n in range(2)] + \
                    [scores_flat[:, n * TOK:(n + 1) * TOK] for n in range(3)]
        tap_free = [()] * len(tap_slots)

        def convolve(b0, ready):
            v_taps, p_taps = [], []
            for k in range(CONV_K):
                for b in range(b0, b0 + 4):
                    if b in V_BLOCKS:
                        v_taps.append(lambda b=b, k=k: v_tap(b, k, ready))
                    else:
                        p_taps.append(lambda b=b, k=k: p_tap(b, k, ready))
            nv, np_ = len(v_taps) // CONV_K, len(p_taps) // CONV_K
            while v_taps or p_taps:
                background.extend(v_taps[:nv])
                background.extend(p_taps[:np_])
                del v_taps[:nv], p_taps[:np_]

        def tap_cols(b, k):
            c = COL_CONV + 8 * k + b
            return conv_in[:, b, k:k + TOK], par[:, c:c + 1], conv_out[:, b, :]

        def v_tap(b, k, ready):
            src, w, out = tap_cols(b, k)
            if k == 0:
                c = ROWS["conv_b"] + b
                conv_did[b] = v_ts(out, src, w, ALU.mult, par[:, c:c + 1], ALU.add, waits=ready)
            else:
                conv_did[b] = v_stt(out, src, w, out, ALU.mult, ALU.add, (conv_did[b],))

        def p_tap(b, k, ready):
            src, w, out = tap_cols(b, k)
            if k == 0:
                c = ROWS["conv_b"] + b
                conv_did[b] = a_affine(out, src, ACT.Identity, w, par[:, c:c + 1], ready)
                return
            s = tap_at[0] % len(tap_slots)
            tap_at[0] += 1
            made = a_copy(tap_slots[s], src, w, tap_free[s])
            conv_did[b] = tt(pool, out, out, tap_slots[s], ALU.add, (made, conv_did[b]))
            tap_free[s] = (conv_did[b],)

        def l0_pool(j):
            def run(ps, done):
                u, u_did = scaled(ps, done)
                p_slot, p_free = take_z()
                pooled = z_flat[p_slot].rearrange("p (c t) -> p c t", c=GK)

                def windows():
                    dids = []
                    for half in range(2):
                        g = 2 * j + half
                        i, free = take_bank()
                        view = bank[i].rearrange("p (k t) -> p k t", k=2)
                        for k in range(2):
                            f = slice((2 * half + k) * P, (2 * half + k + 1) * P)
                            w = u_did + free + band_did[-1:]
                            mm(view[:, k, :], z[:, u, 0, f], band0[:, g, :], True, False, w)
                            did = mm_last(view[:, k, P:], z[:, u, 1, f], band1[:, g, :], False, True)
                        dids.append(a_copy(pooled[:, 2 * half:2 * half + 2, :], view, waits=(did,) + p_free))
                        bank_free[i] = (dids[-1],)
                    z_free[u] = ((pe.sem, pe.sem.value),)
                    gain_read[0] = ((pe.sem, pe.sem.value),)
                    defer(1, lambda: mix(dids))

                def mix(dids):
                    group_ready[("B", j)] = ()
                    for half in range(2):
                        g = 2 * j + half
                        i, free = take_bank()
                        view = bank[i].rearrange("p (k t) -> p k t", k=2)
                        for e_ in range(2):
                            for c in range(2):
                                did = mm_last(view[:, e_, :], pool_w[:, g, c, e_ * P:(e_ + 1) * P],
                                              pooled[:, 2 * half + c, :], c == 0, c == 1,
                                              (dids[half], pool_w_did[0]) + free)
                        at = ROWS["pool_scale"] + 2 * g
                        bank_free[i] = store_scaled("B", 2 * g, view, [par[:, at + c:at + c + 1] for c in range(2)], did)
                    z_free[p_slot] = ((pe.sem, pe.sem.value),)
                    acc_free[0] = ((pe.sem, pe.sem.value),)
                defer(2 - j, windows)
                return u_did
            return run

        ln = {}

        def l0_norm_tile(tt_):
            did_all = tuple(conv_did[b] for b in range(8))
            stats, mean_var, rstd = small_cols(12), small_cols(2), small_cols(1)
            banks = []
            for h in range(2):
                i, free = take_bank()
                for b in range(4):
                    did = transpose(bank[i][:, b * P:(b + 1) * P], conv_out[:, 4 * h + b, tt_ * P:(tt_ + 1) * P],
                                    waits=did_all + free, last=b == 3)
                banks.append(i)
                stat_did = dve.op(lambda e, o=stats[:, 6 * h:6 * h + 6], s=bank[i]: e.bn_stats(o, s), (did,))
            aggr_did = dve.op(lambda e: e.bn_aggr(mean_var, stats), (stat_did,))
            r_did = inv_sqrt(rstd, mean_var[:, 1:2], 1, (aggr_did,))
            s, free = take_z()
            for h in range(2):
                did = v_ts(z_flat[s][:, h * CH:(h + 1) * CH], bank[banks[h]], mean_var[:, 0:1], ALU.subtract,
                           rstd, ALU.mult, waits=(r_did,) + free)
                bank_free[banks[h]] = (did,)
            ln[tt_] = (s, did)
            if tt_ + 1 < NT:
                defer(1, lambda: l0_norm_tile(tt_ + 1))
            else:
                defer(2, lambda: l0_silu(0))

        def l0_silu(j):
            did_all = tuple(conv_did[b] for b in range(8))
            slots, n_did = [ln[tt_][0] for tt_ in range(NT)], [ln[tt_][1] for tt_ in range(NT)]
            work = conv_in_flat
            parts = []
            group_ready[("B", 2 + j)] = ()

            def evacuate(half, view, done):
                a = work[:, half * CH:(half + 1) * CH].rearrange("p (k t) -> p k t", k=2)
                s = work[:, D // 2 + half * CH:D // 2 + (half + 1) * CH].rearrange("p (k t) -> p k t", k=2)
                for k in range(2):
                    b = GK * j + 2 * half + k
                    g_, b_ = (par[:, ROWS[n] + b:ROWS[n] + b + 1] for n in ("ln_g", "ln_b"))
                    a_did = v_ts(a[:, k, :], view[:, k, :], g_, ALU.mult, b_, ALU.add,
                                 waits=(done,) + state.get(("silu", half), did_all))
                for k in range(2):
                    b = GK * j + 2 * half + k
                    g_, b_ = (par[:, ROWS[n] + b:ROWS[n] + b + 1] for n in ("ln_g", "ln_b"))
                    s_did = a_affine(s[:, k, :], view[:, k, :], ACT.Sigmoid, g_, b_, (a_did,))
                parts.append((half, a, s, (a_did, s_did)))
                return (a_did, s_did)
            to_features(lambda tt_: z_flat[slots[tt_]][:, j * CH:(j + 1) * CH], tuple(n_did), evacuate)
            for half, a, s, did in parts:
                y_did = tt(dve, a, a, s, ALU.mult, did)
                state[("silu", half)] = store_halves(
                    "B", GK * (2 + j) + 2 * half, 2,
                    lambda hi, w: a_copy(hi, a, waits=w + (y_did,)),
                    lambda lo, hi, w: tt(dve, lo, a, hi, ALU.subtract, w))
            if j == 0:
                defer(1, lambda: l0_silu(1))
            else:
                for s in slots:
                    z_free[s] = ((pe.sem, pe.sem.value),)
                state["conv_free"] = state[("silu", 0)] + state[("silu", 1)] + ((pe.sem, pe.sem.value),)

        def l0_flush():
            run_background(everything=True)
            run_due(everything=True)

        w = t["ab_w_in"][0]
        for j in range(2):
            product(w, 0, 16, D_POOL + j * CH, "A", 0, l0_value,
                    (lambda: (begin(FIRST_COL, split_first), defer(5, lambda: turn_rows(rows_did[0])))) if j == 0 else
                    (lambda: (load_pool_w(), per_step.__setitem__(0, CONV_PER_STEP))))
            product(w, 0, 16, D_POOL + D_CONV + j * CH, "A", 0, l0_gate(j))
        for j in range(2):
            product(w, 0, 16, j * CH, "A", 0, l0_pool(j))
        w = t["ab_w_out"][0]

        def l0_out_first(n):
            return lambda ps, done: add_block(n, True, ps, done)

        def finish(n, alone):
            return lambda ps, done, tiles=(0, 1): finish_block(n, ps, done, alone, tiles)

        for n in range(NG):
            product(w, 0, 8, n * CH, "B", 0, l0_out_first(n),
                    (lambda: load_gain(t["mix_post_g"][0])) if n == 1 else None)
        for n in range(NG):
            product(w, D_POOL, 8, n * CH, "B", 2, finish(n, False), l0_flush if n == 0 else None, n == NG - 1)

        def mlp(layer):
            w1, w2 = t["ffn_w1"][layer], t["ffn_w2"][layer]
            n_blocks = D_FF // FF_BLOCK

            def hidden(group):
                def run(ps, done):
                    s, r_did = scaled(ps, done, ACT.Relu)
                    dids = tuple(tt(pool, z[:, s, tt_, :], z[:, s, tt_, :], z[:, s, tt_, :], ALU.mult, (r_did[tt_],))
                                 for tt_ in range(NT))

                    def turn():
                        to_features(lambda tt_: z[:, s, tt_, :], dids, split_plain("B", group))
                        z_free[s] = ((pe.sem, pe.sem.value),)
                    defer(2, turn)
                    return r_did
                return run

            def up(b):
                for j in range(2):
                    before = None
                    if (b, j) == (0, 0):
                        before = lambda: begin(ROWS[f"ffn_pre{layer}"])
                    elif (b, j) == (0, 1):
                        before = lambda: load_gain(t["ffn_post_g"][layer])
                    product(w1, 0, 16, b * FF_BLOCK + j * CH, "A", 0, hidden((2 * b + j) % NG), before)

            def down(b):
                for n in range(NG):
                    if b == n_blocks - 1:
                        done = finish(n, False)
                    else:
                        done = (lambda n: lambda ps, did: add_block(n, b == 0, ps, did))(n)
                    product(w2, b * FF_BLOCK, 8, n * CH, "B", (2 * b) % NG, done,
                            by_token=(b, n) == (n_blocks - 1, NG - 1))

            up(0)
            for b in range(1, n_blocks):
                up(b)
                down(b - 1)
            down(n_blocks - 1)

        mlp(0)

        short_in = conv_in_flat[:, 0:GK * (TOK + SHORT_K - 1)].rearrange("p (b t) -> p b t", b=GK)
        short_out = conv_out_flat[:, 0:GK * TOK].rearrange("p (b t) -> p b t", b=GK)
        SPAD = SHORT_K - 1

        def l1_start():
            begin(ROWS["mix_pre1"])
            state["spad"] = (pool.op(lambda e: e.memset(short_in[:, :, 0:SPAD], 0.0), state["conv_free"]),)
            state["short_free"] = ()
            state["y_free"] = ()

        def l1_c(ps, done):
            state["c"] = scaled(ps, done)
            return state["c"][1]

        def l1_u(j):
            def run(ps, done):
                c, c_did = state["c"]
                dids = tuple(v_stt(z[:, c, tt_, :], ps[tt_], rs[0][:, tt_:tt_ + 1], z[:, c, tt_, :], ALU.mult,
                                   ALU.mult, (done, c_did[tt_])) for tt_ in range(NT))

                def turn():
                    out = []

                    def evacuate(half, view, did):
                        out.append(a_copy(short_in[:, 2 * half:2 * half + 2, SPAD:], view,
                                          waits=(did,) + state["spad"] + state["short_free"]))
                        return out[-1:]
                    to_features(lambda tt_: z[:, c, tt_, :], dids, evacuate)
                    z_free[c] = ((pe.sem, pe.sem.value),)
                    did = None
                    for b in range(GK):
                        for k in range(SHORT_K):
                            col = COL_SHORT + k * (D // P) + GK * j + b
                            src, wk, o = short_in[:, b, k:k + TOK], par[:, col:col + 1], short_out[:, b, :]
                            if k == 0:
                                did = v_ts(o, src, wk, ALU.mult, waits=tuple(out) + state["y_free"])
                            else:
                                did = v_stt(o, src, wk, o, ALU.mult, ALU.add, (did,))
                    state["short_did"] = did
                    state["short_free"] = (did,)
                defer(2, turn)
                return dids
            return run

        def l1_b(j):
            def run(ps, done):
                b, b_did = scaled(ps, done)

                def turn():
                    group_ready[("B", j)] = ()
                    free = []

                    def evacuate(half, view, did):
                        y = short_out[:, 2 * half:2 * half + 2, :]
                        y_did = tt(dve, y, view, y, ALU.mult, (did, state["short_did"]))
                        free.extend(store_halves(
                            "B", GK * j + 2 * half, 2,
                            lambda hi, w: a_copy(hi, y, waits=w + (y_did,)),
                            lambda lo, hi, w: tt(dve, lo, y, hi, ALU.subtract, w)))
                        return (y_did,)
                    to_features(lambda tt_: z[:, b, tt_, :], b_did, evacuate)
                    z_free[b] = ((pe.sem, pe.sem.value),)
                    state["y_free"] = tuple(free)
                defer(2, turn)
                return b_did
            return run

        w = t["sc_w_in"][0]
        for j in range(NG):
            product(w, 0, 16, D + j * CH, "A", 0, l1_c,
                    l1_start if j == 0 else (lambda: load_gain(t["mix_post_g"][1])) if j == 1 else None)
            product(w, 0, 16, 2 * D + j * CH, "A", 0, l1_u(j))
            product(w, 0, 16, j * CH, "A", 0, l1_b(j))
        w = t["sc_w_out"][0]
        for n in range(NG):
            product(w, 0, 16, n * CH, "B", 0, finish(n, True), by_token=n == NG - 1)
        mlp(1)

        W_ATT = HEADS * HD
        q_T = acc_flat[:, 0:HEADS * TOK].rearrange("p (h t) -> p h t", h=HEADS)
        k_T = acc_flat[:, HEADS * TOK:2 * HEADS * TOK].rearrange("p (h t) -> p h t", h=HEADS)
        v_tok = gain_row.rearrange("p (t c) -> p t c", t=NT)
        att = conv_out_flat.rearrange("p (t c) -> p t c", t=NT)
        vg = conv_in_flat[:, 0:NT * W_ATT].rearrange("p (t c) -> p t c", t=NT)
        ws_T = ws_flat.rearrange("p (g c) -> p g c", g=HEADS)
        merged = acc
        HPC = CH // HD

        def l2_start():
            begin(ROWS["pre2"])
            state["pt"] = []

        def l2_spatial():
            s, free = take_z()
            raw = z_flat[s].rearrange("p (g c) -> p g c", g=HEADS)
            did = sp.dma(raw, t["w_spatial_2"][0].rearrange("g t s -> t g s"), ws_loaded, free)
            def turn():
                kept = pool.op(lambda e: e.affine_select(out=raw, in_=raw, compare_op=ALU.is_ge, fill=0.0, base=0,
                                                        pattern=[[0, HEADS], [-1, P]], channel_multiplier=1), (did, sgu_did[0]))
                for h in range(2):
                    i, bfree = take_bank()
                    for g in range(4):
                        tr = transpose(bank[i][:, g * P:(g + 1) * P], raw[:, 4 * h + g, :], waits=(kept,) + bfree, last=g == 3)
                    ws_did = a_copy(ws_flat[:, h * CH:(h + 1) * CH], bank[i], waits=(tr,))
                    bank_free[i] = (ws_did,)
                state["ws_did"] = ws_did
                z_free[s] = (tr,)
            defer(3, turn)

        def heads_norm(src, dids, then):
            tmp, free = take_z()
            sums, factors = small_cols(NT * HPC), small_cols(NT * HPC)

            def squares():
                sq = a_copy(z[:, tmp, :, :], src, 1.0, dids + free, ACT.Square)
                defer(1, lambda: total(sq))

            def total(sq):
                s_did = dve.op(lambda e: e.reduce_sum(sums.rearrange("p (t h) -> p t h", t=NT),
                                                      z[:, tmp, :, :].rearrange("p t (h c) -> p t h c", h=HPC),
                                                      axis=AXIS.X), (sq,))
                z_free[tmp] = (s_did,)
                f_did = inv_sqrt(factors, sums, HD, (s_did,))
                defer(2, lambda: scale(f_did))

            def scale(f_did):
                for tt_ in range(NT):
                    v3 = src[:, tt_, :].rearrange("p (h c) -> p h c", h=HPC)
                    f3 = factors[:, tt_ * HPC:(tt_ + 1) * HPC].unsqueeze(2).to_broadcast([P, HPC, HD])
                    did = tt(dve, v3, v3, f3, ALU.mult, (f_did,))
                defer(1, lambda: then((did,)))
            defer(0, squares)

        def l2_qk(dst, key, j):
            def run(ps, done):
                s, s_did = scaled(ps, done)
                gain = par[:, ROWS[key]:ROWS[key] + 1]

                def turn(n_did):
                    def evacuate(half, view, did):
                        h = HPC * j + 2 * half
                        state["qk_did"] = a_copy(dst[:, h:h + 2, :], view, gain, (did,) + acc_free[0])
                        return (state["qk_did"],)
                    to_features(lambda tt_: z[:, s, tt_, :], n_did, evacuate)
                    z_free[s] = ((pe.sem, pe.sem.value),)
                heads_norm(z[:, s, :, :], s_did, turn)
                return s_did
            return run

        def l2_v(j):
            def run(ps, done):
                dids = tuple(a_copy(v_tok[:, tt_, j * CH:(j + 1) * CH], ps[tt_], rs[0][:, tt_:tt_ + 1],
                                    (done, rs_did[0]) + gain_read[0]) for tt_ in range(NT))
                state["v_did"] = dids
                return dids
            return run

        def silu_of(ps, done, out, waits=()):
            s_did = tuple(a_copy(out[tt_], ps[tt_], rs[0][:, tt_:tt_ + 1], (done, rs_did[0]) + tuple(waits), ACT.Sigmoid)
                          for tt_ in range(NT))
            return tuple(v_stt(out[tt_], ps[tt_], rs[0][:, tt_:tt_ + 1], out[tt_], ALU.mult, ALU.mult, (s_did[tt_],))
                         for tt_ in range(NT))

        def l2_za(j):
            def run(ps, done):
                dids = silu_of(ps, done, [att[:, tt_, j * CH:(j + 1) * CH] for tt_ in range(NT)], state["y_free"])
                state[("za", j)] = dids
                if j == 1:
                    defer(1, attention)
                return dids
            return run

        scores_buf = scores_flat.rearrange("p (s c) -> p s c", s=2)
        probs_T = prod_rows
        score_free = {0: (), 1: ()}
        probs_T_free = [()]
        head = {}

        def att_scores(h):
            i, free = take_bank()
            ps = bank[i]
            ready = (state["qk_did"], mask_did) + free
            mm(ps[:, 0:TOK], q_T[:, h, P:TOK], k_T[:, h, :], True, True, ready)
            did = mm_last(ps[:, TOK:3 * P], q_T[:, h, 0:P], k_T[:, h, 0:P], True, True)
            s = scores_buf[:, h % 2, :]
            m_did = tt(dve, s, ps[:, 0:3 * P], mask, ALU.add, (did,) + score_free[h % 2])
            bank_free[i] = (m_did,)
            top, bias, total, inv = small_cols(2), small_cols(2), small_cols(2), small_cols(2)
            parts = (s[:, TOK:3 * P], s[:, 0:TOK])
            t_did = tuple(dve.op(lambda e, o=top[:, n:n + 1], v=parts[n]: e.reduce_max(o, v, axis=AXIS.X), (m_did,))
                          for n in range(2))
            b_did = v_ts(bias, top, -SCALE, ALU.mult, waits=t_did)
            head[h] = (s, parts, bias, total, inv, b_did)

        def att_exp(h):
            s, parts, bias, total, inv, b_did = head[h]
            e_did = tuple(a_sum(parts[n], parts[n], ACT.Exp, total[:, n:n + 1], (b_did,), bias=bias[:, n:n + 1], scale=SCALE)
                          for n in range(2))
            i_did = dve.op(lambda e: e.reciprocal(inv, total), e_did)
            head[h] = (s, inv, e_did, i_did)

        def att_turn(h):
            s, inv, e_did, i_did = head[h]
            i, free = take_bank()
            for b in range(3):
                did = transpose(bank[i][:, b * P:(b + 1) * P], s[:, b * P:(b + 1) * P], waits=e_did + free, last=b == 2)
            score_free[h % 2] = (did,)
            c_did = a_copy(probs_T[:, 0:3 * P], bank[i][:, 0:3 * P], waits=(did,) + probs_T_free[0])
            bank_free[i] = (c_did,)
            head[h] += (c_did,)

        def att_values(h):
            s, inv, e_did, i_did, c_did = head[h]
            i, free = take_bank()
            cols = slice(h * HD, (h + 1) * HD)
            ready = (c_did,) + state["v_did"] + free
            mm(bank[i][:, 0:HD], probs_T[:, 2 * P:3 * P], v_tok[:, 0, cols], True, True, ready)
            mm(bank[i][:, HD:2 * HD], probs_T[:, 0:P], v_tok[:, 0, cols], True, False)
            did = mm_last(bank[i][:, HD:2 * HD], probs_T[:, P:2 * P], v_tok[:, 1, cols], False, True)
            probs_T_free[0] = (did,)
            o_did = tuple(v_stt(att[:, n, cols], bank[i][:, n * HD:(n + 1) * HD], inv[:, n:n + 1], att[:, n, cols],
                                ALU.mult, ALU.mult, (did, i_did) + state[("za", 0)] + state[("za", 1)]) for n in range(2))
            bank_free[i] = o_did
            state[("att", h)] = o_did

        def att_out(j):
            to_features(lambda tt_: att[:, tt_, j * CH:(j + 1) * CH],
                        sum((state[("att", h)] for h in range(HPC * j, HPC * (j + 1))), ()), split_plain("B", j))

        def attention():
            for h in range(HEADS + 1):
                for first, task in ((0, att_scores), (1, att_turn), (0, att_exp), (1, att_values)):
                    if 0 <= h - first < HEADS:
                        background.append(lambda task=task, n=h - first: task(n))
            for j in range(2):
                background.append(lambda j=j: att_out(j))
            per_step[0] = 0.76

        def gelu_into(ps, done, out, waits, then):
            tmp, free = take_z()
            w = z[:, tmp, :, :]
            ready = (done, rs_did[0]) + tuple(waits) + tuple(free)
            v_did, s_did = (), ()
            for tt_ in range(NT):
                f = rs[0][:, tt_:tt_ + 1]
                v_did += (a_copy(out[:, tt_, :], ps[tt_], f, ready),)
                s_did += (a_copy(w[:, tt_, :], ps[tt_], f, ready, ACT.Square),)

            def cubic():
                d = v_ts(w, w, GELU_A, ALU.mult, 1.0, ALU.add, waits=s_did)
                d = tt(dve, w, w, out, ALU.mult, (d,) + v_did)
                defer(1, lambda: sigmoid(d))

            def sigmoid(d):
                d = a_copy(w, w, float(GELU_B), (d,), ACT.Sigmoid)
                defer(1, lambda: product_(d))

            def product_(d):
                d = tt(dve, out, out, w, ALU.mult, (d,))
                z_free[tmp] = (d,)
                then((d,))
            defer(0, cubic)
            return s_did

        def l2_vb(j):
            def run(ps, done):
                out = vg[:, :, j * CH:(j + 1) * CH]

                def gained(n_did):
                    row = sgu_row.unsqueeze(1).to_broadcast([P, HPC, HD])
                    for tt_ in range(NT):
                        v3 = out[:, tt_, :].rearrange("p (h c) -> p h c", h=HPC)
                        did = tt(pool, v3, v3, row, ALU.mult, n_did + (sgu_did[0],))
                    state[("vg", j)] = did
                return gelu_into(ps, done, out, state["short_free"], lambda d: heads_norm(out, d, gained))
            return run

        def l2_ub(j):
            def run(ps, done):
                u, u_free = take_z()

                def mix(g_did):
                    dids = ()
                    for tt_ in range(NT):
                        i, bfree = take_bank()
                        for c in range(HPC):
                            g = HPC * j + c
                            did = mm_last(bank[i][:, c * HD:(c + 1) * HD], ws_T[:, g, :], vg[:, tt_, g * HD:(g + 1) * HD],
                                          True, True, (state["ws_did"], state[("vg", j)]) + bfree)
                        for c in range(HPC):
                            g = HPC * j + c
                            o = z[:, u, tt_, c * HD:(c + 1) * HD]
                            last = v_stt(o, bank[i][:, c * HD:(c + 1) * HD],
                                         par[:, ROWS["b_spatial"] + g:ROWS["b_spatial"] + g + 1], o,
                                         ALU.add, ALU.mult, (did,) + g_did)
                        bank_free[i] = (last,)
                        dids += (last,)
                    state["sgu"] = (u, dids)
                return gelu_into(ps, done, z[:, u, :, :], u_free, mix)
            return run

        def l2_zb(j):
            def run(ps, done):
                tmp, free = take_z()
                zz = [z[:, tmp, tt_, :] for tt_ in range(NT)]
                s_did = silu_of(ps, done, zz, free)
                u, u_did = state["sgu"]
                dids = tuple(tt(pool, z[:, u, tt_, :], z[:, u, tt_, :], zz[tt_], ALU.mult, (u_did[tt_], s_did[tt_]))
                             for tt_ in range(NT))
                z_free[tmp] = dids

                def turn():
                    to_features(lambda tt_: z[:, u, tt_, :], dids, split_plain("B", 2 + j))
                    z_free[u] = ((pe.sem, pe.sem.value),)
                defer(2, turn)
                return s_did
            return run

        def l2_gate(key):
            def run(ps, done):
                state[key] = scaled(ps, done, ACT.Sigmoid)
                return state[key][1]
            return run

        def l2_proj(n, key):
            def run(ps, done):
                g, g_did = state[key]
                cols = slice(n * CH, (n + 1) * CH)
                dids = ()
                for tt_ in range(NT):
                    out = merged[:, tt_, cols]
                    if key == "ga":
                        did = tt(dve, out, ps[tt_], z[:, g, tt_, :], ALU.mult,
                                 (done, g_did[tt_], state["qk_read"]))
                        state[("m", n, tt_)] = did
                        dids += (did,)
                    else:
                        did = tt(dve, z[:, g, tt_, :], ps[tt_], z[:, g, tt_, :], ALU.mult, (done, g_did[tt_]))
                        dids += (did,)
                        state[("m", n, tt_)] = tt(pool, out, out, z[:, g, tt_, :], ALU.add, (did, state[("m", n, tt_)]))
                z_free[g] = dids if key == "ga" else (state[("m", n, 0)], state[("m", n, 1)])
                if key == "gb" and n == NG - 1:
                    for g_ in range(NG):
                        to_features(lambda tt_: merged[:, tt_, g_ * CH:(g_ + 1) * CH],
                                    (state[("m", g_, 0)], state[("m", g_, 1)]), split_plain("A", g_))
                return dids
            return run

        def before_proj():
            run_due(everything=True)
            run_background(everything=True)
            state["qk_read"] = (pe.sem, pe.sem.value)

        out_dram = t["out"].rearrange("b (t p) d -> p (b t) d", p=P)

        def l2_out(n):
            def run(ps, done, tiles=(0, 1)):
                cols = slice(n * CH, (n + 1) * CH)
                dids = ()
                for tt_ in tiles:
                    did = tt(dve, x[:, tt_, cols], ps[tt_], x[:, tt_, cols], ALU.add, (done,) + x_ready[(n, tt_)])
                    sp.dma(out_dram[:, tt_, cols], x[:, tt_, cols], out_written, (did,))
                    dids += (did,)
                return dids
            return run

        w = t["w_in_2"][0]

        def cols_of(part, j):
            return part * W_ATT + j * CH

        GA, GB = 7 * W_ATT, 7 * W_ATT + D
        for j in range(2):
            product(w, 0, 16, cols_of(0, j), "A", 0, l2_qk(q_T, "q_g", j), l2_start if j == 0 else None)
        for j in range(2):
            product(w, 0, 16, cols_of(1, j), "A", 0, l2_qk(k_T, "k_g", j))
        for j in range(2):
            product(w, 0, 16, cols_of(2, j), "A", 0, l2_v(j), l2_spatial if j == 1 else None)
        for j in range(2):
            product(w, 0, 16, cols_of(3, j), "A", 0, l2_za(j))
        for j in range(2):
            product(w, 0, 16, cols_of(5, j), "A", 0, l2_vb(j))
        for j in range(2):
            product(w, 0, 16, cols_of(4, j), "A", 0, l2_ub(j))
            product(w, 0, 16, cols_of(6, j), "A", 0, l2_zb(j))
        for n in range(NG):
            product(w, 0, 16, GA + n * CH, "A", 0, l2_gate("ga"))
            product(w, 0, 16, GB + n * CH, "A", 0, l2_gate("gb"))
            product(t["w_proj_a_2"][0], 0, 8, n * CH, "B", 0, l2_proj(n, "ga"), before_proj if n == 0 else None)
            product(t["w_proj_b_2"][0], 0, 8, n * CH, "B", 2, l2_proj(n, "gb"))
        for n in range(NG):
            product(t["w_out_2"][0], 0, 16, n * CH, "A", 0, l2_out(n), by_token=n == NG - 1)

        steps = [(c, i) for c in chunks for i in range(c["nk"] // STEP_K)]
        STEPS_PER_LOAD = GK // STEP_K
        loads = len(steps) // STEPS_PER_LOAD
        next_load = [0]

        def load_weights(n):
            c, i = steps[n * STEPS_PER_LOAD]
            row = c["row0"] + i * STEP_K * P
            src = c["w"][row:row + GK * P, c["col0"]:c["col0"] + CH].rearrange("(k p) c -> p k c", p=P)
            slot = n % RAW_SLOTS
            used = ((lo_made, STEPS_PER_LOAD * (n - RAW_SLOTS + 1)),) if n >= RAW_SLOTS else ()
            sp.dma(w_raw[:, slot, :].rearrange("p (k c) -> p k c", k=GK), src, raw_loaded[slot], used)

        def split_weights(s):
            n, part = divmod(s, STEPS_PER_LOAD)
            while next_load[0] < loads and next_load[0] <= n + RAW_SLOTS - 1:
                load_weights(next_load[0])
                next_load[0] += 1
            raw = w_raw[:, n % RAW_SLOTS, part * STEP_K * CH:(part + 1) * STEP_K * CH]
            loaded = (raw_loaded[n % RAW_SLOTS], 16 * (n // RAW_SLOTS + 1))
            free = (step_done, s - SPLIT_SLOTS + 1) if s >= SPLIT_SLOTS else None
            slot = s % SPLIT_SLOTS
            hi = a_copy(w_hi[:, slot, :], raw, waits=(loaded, free), sem=hi_made)
            tt(dve, w_lo[:, slot, :], raw, w_hi[:, slot, :].bitcast(F32), ALU.subtract, (hi, free), sem=lo_made)

        pair_free = [(), ()]
        load_x(0)
        first_did = load_first_gain()
        for n in range(RAW_SLOTS):
            load_weights(n)
            load_x(n + 1)
        next_load[0] = RAW_SLOTS
        rows_did[0] = load_rows()
        sgu_did[0] = sp.dma(sgu_row, t["sgu_norm_g_2"].to_broadcast([P, HD]), sgu_loaded)
        turn_first_gain(first_did)
        next_split = [0]

        def split_until(s):
            while next_split[0] <= min(s, len(steps) - 1):
                split_weights(next_split[0])
                next_split[0] += 1

        def step_matmuls(s, ps, tiles, c, i, sem_of):
            hi, lo = halves[c["buf"]]
            slot = s % SPLIT_SLOTS
            n_steps = c["nk"] // STEP_K
            for k in range(STEP_K):
                kt = GK * c["group0"] + i * STEP_K + k
                wh, wl = (v[:, slot, k * CH:(k + 1) * CH] for v in (w_hi, w_lo))
                for tt_ in tiles:
                    tok = slice(tt_ * P, (tt_ + 1) * P)
                    first, last = i == 0 and k == 0, i == n_steps - 1 and k == STEP_K - 1
                    mm(ps[tt_], lo[:, kt, tok], wh, first, False)
                    mm(ps[tt_], hi[:, kt, tok], wl, False, False)
                    if k == STEP_K - 1 and tt_ == tiles[-1]:
                        done = mm_last(ps[tt_], hi[:, kt, tok], wh, False, last, sem=sem_of)
                    else:
                        mm(ps[tt_], hi[:, kt, tok], wh, False, last)
            return done

        pair = -1
        for s, (c, i) in enumerate(steps):
            now[0] = s
            if i == 0:
                pair += 1
                if c["before"]:
                    c["before"]()
            left = c["nk"] // STEP_K - i
            ps = [bank[2 * (pair % 2) + tt_] for tt_ in range(NT)]
            group = c["group0"] + i * STEP_K // GK
            tiles = (0, 1)
            if c["by_token"] and left <= SPLIT_SLOTS:
                tiles = (1,)
                if left == SPLIT_SLOTS:
                    for n in range(SPLIT_SLOTS):
                        split_until(s + n)
                        pe.wait((lo_made, s + n + 1), *group_ready[(c["buf"], c["group0"] + (i + n) * STEP_K // GK)])
                        if i + n == 0:
                            pe.wait(*pair_free[pair % 2])
                        done = step_matmuls(s + n, ps, (0,), c, i + n, pe.sem)
                    tile0_read = tuple(c["done"](ps, done, (0,)))
            split_until(s + AHEAD if tiles != (1,) else min(s + AHEAD, s + left + HELD_AHEAD - 1))
            pe.wait((lo_made, s + 1), *group_ready[(c["buf"], group)])
            if i == 0:
                pe.wait(*pair_free[pair % 2])
            done = step_matmuls(s, ps, tiles, c, i, step_done)
            group_read[(c["buf"], group)] = done
            if left == 1:
                if tiles == (1,):
                    pair_free[pair % 2] = tile0_read + tuple(c["done"](ps, done, (1,)))
                else:
                    pair_free[pair % 2] = tuple(c["done"](ps, done))
            run_due()
            run_background()
        run_due(everything=True)
        sp.wait((out_written, out_written.value))

        block = ctx.enter_context(nc.Block())

        @block.sync
        def _(e):
            sp.replay(e)

        @block.scalar
        def _(e):
            act.replay(e)

        @block.vector
        def _(e):
            dve.replay(e)

        @block.gpsimd
        def _(e):
            pool.replay(e)

        @block.tensor
        def _(e):
            pe.replay(e)


INPUTS = ("x", "mix_pre_g", "mix_post_g", "ffn_pre_g", "ffn_post_g", "ab_w_in", "pool_w", "pool_scale", "conv_w",
          "conv_b", "conv_ln_g", "conv_ln_b", "ab_w_out", "sc_w_in", "sc_conv_w", "sc_w_out", "ffn_w1", "ffn_w2",
          "norm_g_2", "w_in_2", "q_norm_g_2", "k_norm_g_2", "sgu_norm_g_2", "w_spatial_2", "b_spatial_2",
          "w_proj_a_2", "w_proj_b_2", "w_out_2")


def kernel(**inputs):
    import concourse.bacc as bacc
    from concourse.bass_utils import run_bass_kernel_spmd

    nc = bacc.Bacc("TRN2", target_bir_lowering=False, num_devices=1)
    arrays, aps = {}, {}
    for name in INPUTS:
        a = np.ascontiguousarray(inputs[name])
        arrays[f"in_{name}"] = a
        aps[name] = nc.dram_tensor(f"in_{name}", a.shape, mybir.dt.from_np(a.dtype), kind="ExternalInput").ap()
    aps["out"] = nc.dram_tensor("out_x", (1, TOK, D), F32, kind="ExternalOutput").ap()
    build(nc, aps)
    r = run_bass_kernel_spmd(nc, [arrays], core_ids=[0])
    return r.results[0]["out_x"]
```
